# Optimizing a Trainium2 kernel written in Bass

```python
import jax, jax.numpy as jnp
from jax import lax
import numpy as np

D_MODEL = 1024
BATCH = 1
SEQ = 1024
DEPTH = 1

N_META = 16
BLOCK = 128
WINDOW = 128
NORM_EPS = 1e-6

SWA_HEADS = 8
SWA_KV_HEADS = 2
SWA_HEAD_DIM = 64
SWA_GROUP = SWA_HEADS // SWA_KV_HEADS
SWA_WIDTH = SWA_HEADS * SWA_HEAD_DIM
SWA_KV_WIDTH = SWA_KV_HEADS * SWA_HEAD_DIM

MLA_HEADS = 8
MLA_Q_LORA = 256
MLA_KV_LORA = 128
MLA_NOPE_DIM = 64
MLA_ROPE_DIM = 32
MLA_V_DIM = 64
MLA_QK_DIM = MLA_NOPE_DIM + MLA_ROPE_DIM
MLA_WIDTH = MLA_HEADS * MLA_V_DIM
ROPE_THETA = 10000.0

MIX_WIDTH = SWA_WIDTH + MLA_WIDTH
IN_SIZES = (SWA_WIDTH, SWA_KV_WIDTH, SWA_KV_WIDTH, MLA_Q_LORA, MLA_KV_LORA, MLA_ROPE_DIM)
IN_WIDTH = SWA_WIDTH + 2 * SWA_KV_WIDTH + MLA_Q_LORA + MLA_KV_LORA + MLA_ROPE_DIM

N_EXPERTS = 32
TOP_K = 4
D_FF = 1024
SWIGLU_LIMIT = 7.0
SWIGLU_ALPHA = 1.702
MOE_BLOCK = 128

kernel_name = "hymba_swa_mla_moe_encoder_block"

def rms_norm(x, g):
    xf = x.astype(jnp.float32)
    y = xf * lax.rsqrt(jnp.mean(xf * xf, axis=-1, keepdims=True) + NORM_EPS)
    return (y * g.astype(jnp.float32)).astype(x.dtype)

def alibi_slopes(n):
    return jnp.asarray(2.0 ** (-8.0 * np.arange(1, n + 1) / n), dtype=jnp.float32)

def apply_rope(x, pos):
    half = x.shape[-1] // 2
    inv = 1.0 / (ROPE_THETA ** (jnp.arange(half, dtype=jnp.float32) / half))
    ang = pos.astype(jnp.float32)[:, None] * inv[None, :]
    cos = jnp.cos(ang)[None, :, None, :]
    sin = jnp.sin(ang)[None, :, None, :]
    xf = x.astype(jnp.float32)
    x1, x2 = xf[..., :half], xf[..., half:]
    return jnp.concatenate([x1 * cos - x2 * sin, x1 * sin + x2 * cos], axis=-1).astype(x.dtype)

def sink_softmax(s, sink):
    m = jnp.maximum(jnp.max(s, axis=-1, keepdims=True), sink)
    p = jnp.exp(s - m)
    return p / (jnp.sum(p, axis=-1, keepdims=True) + jnp.exp(sink - m))

def _band_attend(q, k, v, dist, valid, slopes, sink):
    scale = SWA_HEAD_DIM ** -0.5
    s = jnp.einsum('bnqkgd,bnskd->bnkgqs', q, k, preferred_element_type=jnp.float32) * scale
    bias = -slopes.reshape(SWA_KV_HEADS, SWA_GROUP)[None, :, :, None, None] * dist[:, None, None].astype(jnp.float32)
    s = jnp.where(valid[:, None, None], s + bias, -jnp.inf)
    p = sink_softmax(s, sink.astype(jnp.float32).reshape(SWA_KV_HEADS, SWA_GROUP)[:, :, None, None])
    return jnp.einsum('bnkgqs,bnskd->bnqkgd', p.astype(v.dtype), v)

def windowed_gqa(q, k, v, sink):
    b, L = q.shape[0], q.shape[1]
    S = L - N_META
    nb = S // BLOCK
    slopes = alibi_slopes(SWA_HEADS)
    km, kr = k[:, :N_META], k[:, N_META:]
    vm, vr = v[:, :N_META], v[:, N_META:]

    qm = q[:, :N_META].reshape(b, 1, N_META, SWA_KV_HEADS, SWA_GROUP, SWA_HEAD_DIM)
    k_mb = jnp.concatenate([km, kr[:, :BLOCK]], axis=1)[:, None]
    v_mb = jnp.concatenate([vm, vr[:, :BLOCK]], axis=1)[:, None]
    d_r = N_META + jnp.arange(BLOCK)[None, :] - jnp.arange(N_META)[:, None]
    dist_m = jnp.concatenate([jnp.zeros((N_META, N_META), jnp.int32), d_r], axis=1)[None]
    valid_m = jnp.concatenate([jnp.ones((N_META, N_META), bool), d_r <= WINDOW], axis=1)[None]
    out_m = _band_attend(qm, k_mb, v_mb, dist_m, valid_m, slopes, sink)

    qr = q[:, N_META:].reshape(b, nb, BLOCK, SWA_KV_HEADS, SWA_GROUP, SWA_HEAD_DIM)

    def band(t_real, t_meta):
        tp = jnp.pad(t_real, ((0, 0), (BLOCK, BLOCK), (0, 0), (0, 0)))
        tp = tp.reshape(b, nb + 2, BLOCK, SWA_KV_HEADS, SWA_HEAD_DIM)
        win = jnp.concatenate([tp[:, :-2], tp[:, 1:-1], tp[:, 2:]], axis=2)
        meta = jnp.broadcast_to(t_meta[:, None], (b, nb, N_META, SWA_KV_HEADS, SWA_HEAD_DIM))
        return jnp.concatenate([meta, win], axis=2)

    qpos = jnp.arange(nb)[:, None] * BLOCK + jnp.arange(BLOCK)[None, :]
    kpos = (jnp.arange(nb)[:, None] - 1) * BLOCK + jnp.arange(3 * BLOCK)[None, :]
    d = jnp.abs(qpos[:, :, None] - kpos[:, None, :])
    in_range = (kpos >= 0) & (kpos < S)
    valid_w = (d <= WINDOW) & in_range[:, None, :]
    dist_r = jnp.concatenate([jnp.zeros((nb, BLOCK, N_META), d.dtype), d], axis=-1)
    valid_r = jnp.concatenate([jnp.ones((nb, BLOCK, N_META), bool), valid_w], axis=-1)
    out_r = _band_attend(qr, band(kr, km), band(vr, vm), dist_r, valid_r, slopes, sink)

    return jnp.concatenate([out_m.reshape(b, N_META, SWA_WIDTH), out_r.reshape(b, S, SWA_WIDTH)], axis=1)

def latent_attention(q_lat, kv_lat, k_rope, q_lat_g, w_q_up, kv_lat_g, w_kv_up, q_g, k_g):
    b, L = q_lat.shape[0], q_lat.shape[1]
    S = L - N_META
    nb = S // BLOCK
    pos = jnp.arange(L)
    q = (rms_norm(q_lat, q_lat_g) @ w_q_up).reshape(b, L, MLA_HEADS, MLA_QK_DIM)
    kv = (rms_norm(kv_lat, kv_lat_g) @ w_kv_up).reshape(b, L, MLA_HEADS, MLA_NOPE_DIM + MLA_V_DIM)
    k_nope, v = kv[..., :MLA_NOPE_DIM], kv[..., MLA_NOPE_DIM:]
    k = jnp.concatenate([k_nope, jnp.broadcast_to(k_rope[:, :, None, :], (b, L, MLA_HEADS, MLA_ROPE_DIM))], axis=-1)
    q = rms_norm(q, q_g)
    k = rms_norm(k, k_g)
    q = jnp.concatenate([q[..., :MLA_NOPE_DIM], apply_rope(q[..., MLA_NOPE_DIM:], pos)], axis=-1)
    k = jnp.concatenate([k[..., :MLA_NOPE_DIM], apply_rope(k[..., MLA_NOPE_DIM:], pos)], axis=-1)
    scale = MLA_QK_DIM ** -0.5

    def attend(qb):
        s = jnp.einsum('bqhd,bshd->bhqs', qb, k, preferred_element_type=jnp.float32) * scale
        p = jax.nn.softmax(s, axis=-1)
        return jnp.einsum('bhqs,bshd->bqhd', p.astype(v.dtype), v)

    out_m = attend(q[:, :N_META]).reshape(b, N_META, MLA_WIDTH)
    qr = q[:, N_META:].reshape(b, nb, BLOCK, MLA_HEADS, MLA_QK_DIM).transpose(1, 0, 2, 3, 4)
    out_r = lax.map(attend, qr)
    out_r = out_r.transpose(1, 0, 2, 3, 4).reshape(b, S, MLA_WIDTH)
    return jnp.concatenate([out_m, out_r], axis=1)

def clamped_swiglu(g, u):
    g = jnp.minimum(g, SWIGLU_LIMIT)
    u = jnp.clip(u, -SWIGLU_LIMIT, SWIGLU_LIMIT)
    return (u + 1.0) * (g * jax.nn.sigmoid(SWIGLU_ALPHA * g))

def moe_ffn(h, router_w, router_b, w_gate, b_gate, w_up, b_up, w_down, b_down):
    T, D = h.shape
    logits = jnp.dot(h, router_w, preferred_element_type=jnp.float32) + router_b.astype(jnp.float32)
    top_logit, top_idx = lax.top_k(logits, TOP_K)
    gate = jax.nn.softmax(top_logit, axis=-1)
    TK = T * TOP_K
    flat_e = top_idx.reshape(TK)
    flat_tok = jnp.repeat(jnp.arange(T, dtype=jnp.int32), TOP_K)
    flat_g = gate.reshape(TK)
    order = jnp.argsort(flat_e)
    se, stok, sg = flat_e[order], flat_tok[order], flat_g[order]
    counts = jnp.bincount(flat_e, length=N_EXPERTS)
    padded = (counts + MOE_BLOCK - 1) // MOE_BLOCK * MOE_BLOCK
    pad_end = jnp.cumsum(padded)
    pad_start = pad_end - padded
    start = jnp.cumsum(counts) - counts
    dest = pad_start[se] + jnp.arange(TK, dtype=jnp.int32) - start[se]
    n_blocks = (TK + N_EXPERTS * (MOE_BLOCK - 1)) // MOE_BLOCK
    P = n_blocks * MOE_BLOCK
    slot_tok = jnp.zeros((P,), jnp.int32).at[dest].set(stok)
    slot_gate = jnp.zeros((P,), jnp.float32).at[dest].set(sg)
    block_e = jnp.minimum(jnp.searchsorted(pad_end, jnp.arange(n_blocks) * MOE_BLOCK, side='right'), N_EXPERTS - 1)
    xs = h[slot_tok].reshape(n_blocks, MOE_BLOCK, D)

    def expert_block(args):
        xb, e = args
        g = xb @ w_gate[e] + b_gate[e]
        u = xb @ w_up[e] + b_up[e]
        return clamped_swiglu(g, u) @ w_down[e] + b_down[e]

    ys = lax.map(expert_block, (xs, block_e)).reshape(P, D)
    ys = (ys.astype(jnp.float32) * slot_gate[:, None]).astype(h.dtype)
    return jnp.zeros_like(h).at[slot_tok].add(ys)

def setup_inputs(seed: int = 0) -> dict:
    key = jax.random.key(seed)
    ks = jax.random.split(key, 24)
    f32 = jnp.float32

    def nrm(k, shape, scale):
        return jax.random.normal(k, shape, f32) * scale

    def gain(k, shape):
        return 1.0 + 0.05 * jax.random.normal(k, shape, f32)

    L = DEPTH
    return {
        "x": nrm(ks[0], (BATCH, SEQ, D_MODEL), 1.0),
        "meta_tokens": nrm(ks[1], (N_META, D_MODEL), 1.0),
        "attn_norm_g": gain(ks[2], (L, D_MODEL)),
        "w_in": nrm(ks[3], (L, D_MODEL, IN_WIDTH), D_MODEL ** -0.5),
        "swa_q_norm_g": gain(ks[4], (L, SWA_HEAD_DIM)),
        "swa_k_norm_g": gain(ks[5], (L, SWA_HEAD_DIM)),
        "swa_sink": nrm(ks[6], (L, SWA_HEADS), 0.5),
        "mla_q_lat_norm_g": gain(ks[7], (L, MLA_Q_LORA)),
        "w_mla_q_up": nrm(ks[8], (L, MLA_Q_LORA, MLA_HEADS * MLA_QK_DIM), MLA_Q_LORA ** -0.5),
        "mla_kv_lat_norm_g": gain(ks[9], (L, MLA_KV_LORA)),
        "w_mla_kv_up": nrm(ks[10], (L, MLA_KV_LORA, MLA_HEADS * (MLA_NOPE_DIM + MLA_V_DIM)), MLA_KV_LORA ** -0.5),
        "mla_q_norm_g": gain(ks[11], (L, MLA_QK_DIM)),
        "mla_k_norm_g": gain(ks[12], (L, MLA_QK_DIM)),
        "w_out": nrm(ks[13], (L, MIX_WIDTH, D_MODEL), MIX_WIDTH ** -0.5),
        "ffn_norm_g": gain(ks[14], (L, D_MODEL)),
        "router_w": nrm(ks[15], (L, D_MODEL, N_EXPERTS), D_MODEL ** -0.5),
        "router_b": nrm(ks[16], (L, N_EXPERTS), 0.01),
        "w_gate": nrm(ks[17], (L, N_EXPERTS, D_MODEL, D_FF), D_MODEL ** -0.5),
        "b_gate": nrm(ks[18], (L, N_EXPERTS, D_FF), 0.01),
        "w_up": nrm(ks[19], (L, N_EXPERTS, D_MODEL, D_FF), D_MODEL ** -0.5),
        "b_up": nrm(ks[20], (L, N_EXPERTS, D_FF), 0.01),
        "w_down": nrm(ks[21], (L, N_EXPERTS, D_FF, D_MODEL), D_FF ** -0.5),
        "b_down": nrm(ks[22], (L, N_EXPERTS, D_MODEL), 0.01),
    }

def reference(x, meta_tokens, attn_norm_g, w_in, swa_q_norm_g, swa_k_norm_g, swa_sink,
              mla_q_lat_norm_g, w_mla_q_up, mla_kv_lat_norm_g, w_mla_kv_up, mla_q_norm_g,
              mla_k_norm_g, w_out, ffn_norm_g, router_w, router_b, w_gate, b_gate, w_up, b_up,
              w_down, b_down):
    b, S, D = x.shape
    meta = jnp.broadcast_to(meta_tokens.astype(x.dtype)[None], (b, N_META, D))
    h = jnp.concatenate([meta, x], axis=1)
    L = h.shape[1]
    split_at = [int(i) for i in np.cumsum(IN_SIZES)[:-1]]
    for l in range(DEPTH):
        a = rms_norm(h, attn_norm_g[l])
        proj = a @ w_in[l]
        q_s, k_s, v_s, q_lat, kv_lat, k_rope = jnp.split(proj, split_at, axis=-1)
        q_s = rms_norm(q_s.reshape(b, L, SWA_HEADS, SWA_HEAD_DIM), swa_q_norm_g[l])
        k_s = rms_norm(k_s.reshape(b, L, SWA_KV_HEADS, SWA_HEAD_DIM), swa_k_norm_g[l])
        v_s = v_s.reshape(b, L, SWA_KV_HEADS, SWA_HEAD_DIM)
        y_a = windowed_gqa(q_s, k_s, v_s, swa_sink[l])
        y_b = latent_attention(q_lat, kv_lat, k_rope, mla_q_lat_norm_g[l], w_mla_q_up[l],
                               mla_kv_lat_norm_g[l], w_mla_kv_up[l], mla_q_norm_g[l], mla_k_norm_g[l])
        h = h + jnp.concatenate([y_a, y_b], axis=-1) @ w_out[l]
        m = rms_norm(h, ffn_norm_g[l]).reshape(b * L, D)
        h = h + moe_ffn(m, router_w[l], router_b[l], w_gate[l], b_gate[l], w_up[l], b_up[l],
                        w_down[l], b_down[l]).reshape(b, L, D)
    return h[:, N_META:]


_drawn_inputs = setup_inputs


def setup_inputs(seed=0):
    import zlib

    import numpy as np

    out = dict(_drawn_inputs(seed))
    spreads = {}
    factors = {'swa_sink': 3.428,
     'mla_q_lat_norm_g': 3.522,
     'mla_q_norm_g': 3.163,
     'mla_k_norm_g': 3.238,
     'b_gate': 8.0,
     'b_up': 8.0,
     'b_down': 8.0,
     'swa_k_norm_g': 2.69}
    for name, (base, spread) in spreads.items():
        noise = np.random.default_rng([zlib.crc32(name.encode()), seed]).standard_normal(out[name].shape)
        drawn = base * np.exp(spread * noise) if base else spread * noise
        out[name] = __import__('jax').numpy.asarray(drawn.astype(out[name].dtype))
    for name, factor in factors.items():
        out[name] = (out[name] * factor).astype(out[name].dtype)
    return out
```

```python
from contextlib import ExitStack

import concourse.bass as bass
from concourse import mybir

F32 = mybir.dt.float32
I32 = mybir.dt.int32
U32 = mybir.dt.uint32
ALU = mybir.AluOpType
ACT = mybir.ActivationFunctionType
AX = mybir.AxisListType

P = 128
D = 1024
SEQ = 1024
META = 16
KEYS = SEQ + META
TILES = SEQ // P
MT = TILES
DC = D // P
EPS = 1e-6

SWA_HEADS, SWA_KV, HD = 8, 2, 64
PAIRS = SWA_HEADS // SWA_KV
BAND = 3 * P + META
MLA_HEADS, NOPE, ROPE, VD = 8, 64, 32, 64
QK = NOPE + ROPE
Q_LORA, KV_LORA = 256, 128
C_K, C_V, C_QL = 512, 640, 768
C_KVL, C_KR, C_END = 1024, 1152, 1184
PROJ = [(0, 512), (512, 1024), (1024, C_END)]

E, TOPK, FF = 32, 4, 1024
FC = FF // P
SLOTS = 160
HALF = SLOTS // 2
ROUNDS = -(-SEQ // SLOTS)
BLOCKS = (SEQ * TOPK - E) // SLOTS + E
LEAST = -(-SEQ * TOPK // SLOTS)
LIMIT, ALPHA = 7.0, 1.702


def rows(t):
    return P if t < MT else META


def cols(t):
    return slice(t * P, t * P + rows(t))


def spread(ap, n):
    return ap.unsqueeze(2).to_broadcast([ap.shape[0], ap.shape[1], n])


def repeat(ap, n):
    return ap.unsqueeze(1).to_broadcast([ap.shape[0], n, ap.shape[1]])


class Mem:

    def __init__(self, nc, ctx):
        self.nc, self.ctx = nc, ctx

    def sb(self, name, shape, dt=F32):
        return self.ctx.enter_context(self.nc.sbuf_tensor(name, shape, dt))

    def ps(self, name, shape):
        return self.ctx.enter_context(self.nc.psum_tensor(name, shape, F32))

    def sem(self, name):
        return self.ctx.enter_context(self.nc.semaphore(name))


def chain(eng, sem):
    count = [0]

    def link(ins):
        count[0] += 1
        ins.then_inc(sem, 1)
        eng.wait_ge(sem, count[0])

    return link


def project(nc, io, keep):
    with ExitStack() as ctx:
        m = Mem(nc, ctx)
        w_in = m.sb("w_in_sb", [P, DC, C_END])
        w_qup = m.sb("w_qup", [P, Q_LORA // P, MLA_HEADS * QK])
        w_kvup = m.sb("w_kvup", [P, MLA_HEADS * (NOPE + VD)])
        g_attn = m.sb("g_attn", [P, DC])
        g_ql = m.sb("g_ql", [P, Q_LORA // P])
        g_kvl = m.sb("g_kvl", [P, 1])
        swa_g = m.sb("swa_g", [P, 2])
        mla_g = m.sb("mla_g", [QK, 2])
        g_rot = m.sb("g_rot", [P, 2, ROPE])
        cos_q = m.sb("cos_q", [P, MT, ROPE])
        sin_q = m.sb("sin_q", [P, MT, ROPE])
        cos_k = m.sb("cos_k", [P, MT + 1, ROPE])
        sin_k = m.sb("sin_k", [P, MT + 1, ROPE])
        inv_n = m.sb("inv_n", [P, 12])
        xt = m.sb("xt", [P, 3, D])
        square = m.sb("square", [P, D], mybir.dt.bfloat16)
        normT = m.sb("normT", [P, 2, DC, P])
        proj = m.sb("proj", [P, 2, C_END])
        proj_sq = m.sb("proj_sq", [P, C_END])
        up_sq = proj_sq[:, 0:MLA_HEADS * QK].rearrange("p (h c) -> p h c", c=QK)
        x_stat = m.sb("x_stat", [P, MT + 1, 3])
        stat = m.sb("stat", [P, 12])
        stat_root = m.sb("stat_root", [P, 12])
        stat_inv = stat_root
        kr_sq = m.sb("kr_sq", [P, 1])
        qn = m.sb("qn", [P, PAIRS, SWA_KV, HD])
        lat = m.sb("lat", [P, 4, P])
        latT = m.sb("latT", [P, 3, P])
        k_raw = m.sb("k_raw", [P, MLA_HEADS, QK])
        q_raw = m.sb("q_raw", [P, MLA_HEADS, QK])
        head_stat = m.sb("head_stat", [P, 2 * MLA_HEADS])
        head_root = m.sb("head_root", [P, 2 * MLA_HEADS])
        head_inv = head_root
        k_rot = m.sb("k_rot", [P, ROPE])
        k_rot2 = proj_sq[:, 0:ROPE]
        wide = MLA_HEADS * ROPE
        q_rot = proj_sq[:, MLA_HEADS * QK:MLA_HEADS * QK + wide].rearrange("p (h c) -> p h c", c=ROPE)
        q_rot2 = proj_sq[:, 0:wide].rearrange("p (h c) -> p h c", c=ROPE)
        xT_bank = m.ps("xT_bank", [P, 2, 512])
        proj_bank = m.ps("proj_bank", [P, 3, 512])
        job_bank = m.ps("job_bank", [P, 3, 512])
        swa_qT, swa_kT, swa_v = keep["swa_qT"], keep["swa_kT"], keep["swa_v"]
        mla_qT, mla_kT, mla_v = keep["mla_qT"], keep["mla_kT"], keep["mla_v"]
        ident = keep["ident"]

        const_in = m.sem("const_in")
        w_in_in = m.sem("w_in_in")
        gains_one = m.sem("gains_one")
        x_in = [m.sem(f"x_in{i}") for i in range(3)]
        x_root = m.sem("x_root")
        x_normed = m.sem("x_normed")
        w_scaled = m.sem("w_scaled")
        xT_done = m.sem("xT_done")
        normT_lo = m.sem("normT_lo")
        normT_hi = m.sem("normT_hi")
        proj_done = m.sem("proj_done")
        proj_out = m.sem("proj_out")
        v_copied = m.sem("v_copied")
        stat_ready = m.sem("stat_ready")
        root_ready = m.sem("root_ready")
        lat_ready = m.sem("lat_ready")
        head_stat_ready = m.sem("head_stat_ready")
        head_root_ready = m.sem("head_root_ready")
        k_ready = m.sem("k_ready")
        q_ready = m.sem("q_ready")
        job_done = m.sem("job_done")
        job_out = m.sem("job_out")
        act_own = m.sem("act_own_p")
        dve_own = m.sem("dve_own_p")
        pool_own = m.sem("pool_own_p")

        jobs = []
        for t in range(MT + 1):
            names = ("qpairs", "lats", "kv0", "kv1", "q0", "q1", "kT0", "kT1", "qT0", "qT1")
            jobs += [(t, n) for n in names if t < MT or n in ("lats", "kv0", "kv1", "kT0", "kT1")]
        place = {job: j for j, job in enumerate(jobs)}

        consts = [
            (g_attn[:], io["attn_norm_g"][0].rearrange("(k p) -> p k", p=P)),
            (g_ql[:], io["mla_q_lat_norm_g"][0].rearrange("(k p) -> p k", p=P)),
            (g_kvl[:], io["mla_kv_lat_norm_g"][0].rearrange("(k p) -> p k", p=P)),
            (swa_g[0:HD, 0:1], io["swa_q_norm_g"][0].rearrange("(k p) -> p k", p=HD)),
            (swa_g[HD:P, 0:1], io["swa_q_norm_g"][0].rearrange("(k p) -> p k", p=HD)),
            (swa_g[0:HD, 1:2], io["swa_k_norm_g"][0].rearrange("(k p) -> p k", p=HD)),
            (swa_g[HD:P, 1:2], io["swa_k_norm_g"][0].rearrange("(k p) -> p k", p=HD)),
            (g_rot[:, 0, :], io["mla_q_norm_g"][0, NOPE:QK].partition_broadcast(P)),
            (g_rot[:, 1, :], io["mla_k_norm_g"][0, NOPE:QK].partition_broadcast(P)),
            (cos_k[:], io["cos2"]),
            (sin_k[:], io["sin2"]),
            (inv_n[:], io["inv_n"]),
            (ident[:], io["ident"]),
            (w_qup[:], io["w_mla_q_up"][0].rearrange("(k p) n -> p k n", p=P)),
            (w_kvup[:], io["w_mla_kv_up"][0]),
        ]
        gain_cols = [
            (mla_g[0:NOPE, 0:1], io["mla_q_norm_g"][0, 0:NOPE].rearrange("(k p) -> p k", p=NOPE)),
            (mla_g[0:NOPE, 1:2], io["mla_k_norm_g"][0, 0:NOPE].rearrange("(k p) -> p k", p=NOPE)),
        ]
        CONSTS = 16 * (len(consts) + len(gain_cols))

        with nc.Block() as block:

            @block.sync
            def _(sp):
                def load_x(t):
                    if t >= 3:
                        sp.wait_ge(xT_done, 2 * (t - 2))
                    src = io["meta_tokens"] if t == MT else io["x"][0, t * P:(t + 1) * P, :]
                    sp.dma_start(xt[0:rows(t), t % 3, :], src).then_inc(x_in[t % 3], 16)

                load_x(0)
                sp.dma_start(w_in[:], io["w_in"][0].rearrange("(k p) n -> p k n", p=P)).then_inc(w_in_in, 16)
                for t in range(1, MT + 1):
                    load_x(t)

            @block.gpsimd
            def _(pool):
                nc.gpsimd.memset(mla_g[:], 1.0).then_inc(gains_one, 1)
                for t in range(MT + 1):
                    n = rows(t)
                    pool.wait_ge(proj_out, 3 * t + 2)
                    nc.gpsimd.tensor_copy(swa_v[0:n, t, :], proj[0:n, t % 2, C_V:C_QL]).then_inc(v_copied, 1)

            @block.scalar
            def _(act):
                link = chain(act, act_own)
                with nc.allow_non_contiguous_dma(reason="gains to one per partition, a few KiB in all"):
                    for dst, src in consts:
                        act.dma_start(dst, src).then_inc(const_in, 16)
                    act.wait_ge(gains_one, 1)
                    for dst, src in gain_cols:
                        act.dma_start(dst, src).then_inc(const_in, 16)

                def x_stats(t):
                    n = rows(t)
                    act.wait_ge(x_in[t % 3], 16 * (t // 3 + 1))
                    link(nc.scalar.activation(square[0:n, :], xt[0:n, t % 3, :], ACT.Square,
                                              accum_out=x_stat[0:n, t, 0:1]))
                    nc.scalar.activation(x_stat[0:n, t, 1:2], x_stat[0:n, t, 0:1], ACT.Sqrt,
                                         scale=1.0 / D, bias=keep["eps"][0:n, :]).then_inc(x_root, 1)

                def proj_copy(t, part):
                    n = rows(t)
                    c0, c1 = PROJ[part]
                    if part == 0 and t >= 2:
                        act.wait_ge(lat_ready, t - 1)
                        act.wait_ge(v_copied, t - 1)
                    act.wait_ge(proj_done, 3 * t + part + 1)
                    nc.scalar.copy(proj[0:n, t % 2, c0:c1], proj_bank[0:n, part, 0:c1 - c0]).then_inc(proj_out, 1)

                def job(t, name):
                    j, n = place[t, name], rows(t)
                    bank = job_bank[:, j % 3, :]
                    act.wait_ge(job_done, j + 1)
                    h = 4 * int(name[-1]) if name[-1] in "01" else 0
                    if name == "qpairs":
                        last = nc.scalar.activation(
                            swa_qT[:, :, cols(t)], bank.rearrange("p (j q) -> p j q", q=P),
                            ACT.Copy, scale=swa_g[:, 0:1])
                    elif name == "lats":
                        nc.scalar.copy(swa_kT[:, cols(t)], bank[:, 0:n])
                        a = 0 if t < MT else 2
                        last = nc.scalar.copy(latT[:, a:3, 0:n],
                                              bank.rearrange("p (j q) -> p j q", q=P)[:, 1 + a:4, 0:n])
                    elif name in ("kv0", "kv1"):
                        kv = bank.rearrange("p (h c) -> p h c", c=NOPE + VD)
                        nc.scalar.copy(k_raw[0:n, h:h + 4, 0:NOPE], kv[0:n, :, 0:NOPE])
                        last = nc.scalar.copy(mla_v[0:n, t, h:h + 4, :], kv[0:n, :, NOPE:NOPE + VD])
                    elif name in ("q0", "q1"):
                        last = nc.scalar.copy(q_raw[:, h:h + 4, :],
                                              bank[:, 0:4 * QK].rearrange("p (h c) -> p h c", c=QK))
                    elif name in ("kT0", "kT1"):
                        last = nc.scalar.copy(mla_kT[:, h:h + 4, cols(t)],
                                              bank.rearrange("p (h q) -> p h q", q=P)[0:QK, :, 0:n])
                    else:
                        last = nc.scalar.activation(
                            mla_qT[:, h:h + 4, cols(t)], bank.rearrange("p (h q) -> p h q", q=P)[0:QK, :, :],
                            ACT.Copy, scale=mla_g[:, 0:1])
                    last.then_inc(job_out, 1)

                x_stats(0)
                for s in range(-1, MT + 1):
                    if s + 2 <= MT:
                        x_stats(s + 2)
                    if s + 1 <= MT:
                        t = s + 1
                        if t >= 2:
                            act.wait_ge(proj_done, 3 * (t - 1))
                        act.wait_ge(xT_done, 2 * t + 1)
                        nc.scalar.copy(normT[:, t % 2, 0:4, 0:rows(t)],
                                       xT_bank[:, 0, :].rearrange("p (k q) -> p k q", q=P)[:, :, 0:rows(t)])\
                            .then_inc(normT_lo, 1)
                    if s >= 0:
                        n = rows(s)
                        act.wait_ge(stat_ready, s + 1)
                        nc.scalar.activation(stat_root[0:n, :], stat[0:n, :], ACT.Sqrt,
                                             bias=keep["eps"][0:n, :]).then_inc(root_ready, 1)
                        if s < MT:
                            if s == 0:
                                act.wait_ge(w_scaled, 1)
                            job(s, "qpairs")
                        job(s, "lats")
                    if s + 1 <= MT:
                        proj_copy(s + 1, 0)
                    if s >= 0:
                        for name in ("kv0", "kv1") + (("q0", "q1") if s < MT else ()):
                            job(s, name)
                        n = rows(s)
                        act.wait_ge(head_stat_ready, s + 1)
                        nc.scalar.activation(head_root[0:n, :], head_stat[0:n, :], ACT.Sqrt,
                                             bias=keep["eps"][0:n, :]).then_inc(head_root_ready, 1)
                    if s + 1 <= MT:
                        proj_copy(s + 1, 1)
                        proj_copy(s + 1, 2)
                    if s >= 0:
                        for name in ("kT0", "kT1") + (("qT0", "qT1") if s < MT else ()):
                            job(s, name)

            @block.vector
            def _(dve):
                link = chain(dve, dve_own)
                v = nc.vector

                def x_norm(t):
                    n = rows(t)
                    dve.wait_ge(x_root, t + 1)
                    link(v.reciprocal(x_stat[0:n, t, 2:3], x_stat[0:n, t, 1:2]))
                    v.tensor_scalar(xt[0:n, t % 3, :], xt[0:n, t % 3, :], x_stat[0:n, t, 2:3], None,
                                    ALU.mult).then_inc(x_normed, 1)

                x_norm(0)
                dve.wait_ge(const_in, CONSTS)
                link(v.tensor_tensor(swa_g[:, 0:1], swa_g[:, 0:1], swa_g[:, 1:2], ALU.mult))
                v.tensor_scalar(swa_g[:, 0:1], swa_g[:, 0:1], float(HD) ** -0.5, None, ALU.mult)
                link(v.tensor_tensor(mla_g[:, 0:1], mla_g[:, 0:1], mla_g[:, 1:2], ALU.mult))
                v.tensor_scalar(mla_g[:, 0:1], mla_g[:, 0:1], float(QK) ** -0.5, None, ALU.mult)
                half = ROPE // 2
                for i, (c, s, n) in enumerate(((cos_q, sin_q, MT), (cos_k, sin_k, MT + 1))):
                    v.tensor_tensor(c[:], cos_k[:, 0:n, :], repeat(g_rot[:, i, :], n), ALU.mult)
                    v.tensor_tensor(s[:, :, 0:half], sin_k[:, 0:n, 0:half], repeat(g_rot[:, i, half:ROPE], n), ALU.mult)
                    link(v.tensor_tensor(s[:, :, half:ROPE], sin_k[:, 0:n, half:ROPE],
                                         repeat(g_rot[:, i, 0:half], n), ALU.mult))
                v.memset(head_stat[:], 1.0)
                for k in range(Q_LORA // P):
                    v.tensor_scalar(w_qup[:, k, :], w_qup[:, k, :], g_ql[:, k:k + 1], None, ALU.mult)
                v.tensor_scalar(w_kvup[:], w_kvup[:], g_kvl[:, 0:1], None, ALU.mult)
                dve.wait_ge(w_in_in, 16)
                for k in range(DC):
                    last = v.tensor_scalar(w_in[:, k, :], w_in[:, k, :], g_attn[:, k:k + 1], None, ALU.mult)
                last.then_inc(w_scaled, 1)

                def rotate(out, tmp, src, cos, sin):
                    v.tensor_tensor(out, src, cos, ALU.mult)
                    lo, hi = (slice(None),) * (len(src.shape) - 1) + (slice(0, half),), \
                        (slice(None),) * (len(src.shape) - 1) + (slice(half, ROPE),)
                    v.tensor_tensor(tmp[lo], src[hi], sin[lo], ALU.mult)
                    link(v.tensor_tensor(tmp[hi], src[lo], sin[hi], ALU.mult))
                    link(v.tensor_tensor(out, out, tmp, ALU.add))

                for s in range(-1, MT + 1):
                    if s + 2 <= MT:
                        x_norm(s + 2)
                    if s + 1 <= MT:
                        t = s + 1
                        if t >= 2:
                            dve.wait_ge(proj_done, 3 * (t - 1))
                        dve.wait_ge(xT_done, 2 * t + 2)
                        v.tensor_copy(normT[:, t % 2, 4:8, 0:rows(t)],
                                      xT_bank[:, 1, :].rearrange("p (k q) -> p k q", q=P)[:, :, 0:rows(t)])\
                            .then_inc(normT_hi, 1)
                    if s < 0:
                        continue
                    n = rows(s)
                    pr = proj[0:n, s % 2, :]
                    dve.wait_ge(proj_out, 3 * (s + 1))
                    if s >= 1:
                        dve.wait_ge(q_ready, s)
                    link(v.tensor_tensor(proj_sq[0:n, :], pr, pr, ALU.mult))
                    v.tensor_reduce(stat[0:n, 0:10], proj_sq[0:n, 0:C_V].rearrange("p (h c) -> p h c", c=HD),
                                    AX.X, ALU.add)
                    v.tensor_reduce(stat[0:n, 10:11], proj_sq[0:n, C_QL:C_KVL], AX.X, ALU.add)
                    v.tensor_reduce(stat[0:n, 11:12], proj_sq[0:n, C_KVL:C_KR], AX.X, ALU.add)
                    link(v.tensor_reduce(kr_sq[0:n, :], proj_sq[0:n, C_KR:C_END], AX.X, ALU.add))
                    v.tensor_tensor(stat[0:n, :], stat[0:n, :], inv_n[0:n, :], ALU.mult).then_inc(stat_ready, 1)
                    rotate(k_rot[0:n, :], k_rot2[0:n], pr[:, C_KR:C_END], cos_k[0:n, s, :], sin_k[0:n, s, :])
                    dve.wait_ge(root_ready, s + 1)
                    link(v.reciprocal(stat_inv[0:n, :], stat_root[0:n, :]))
                    if s < MT:
                        for g in range(SWA_KV):
                            v.tensor_tensor(
                                qn[:, :, g, :],
                                pr[:, g * PAIRS * HD:(g + 1) * PAIRS * HD].rearrange("p (j c) -> p j c", c=HD),
                                spread(stat_inv[:, g * PAIRS:(g + 1) * PAIRS], HD), ALU.mult)
                        v.tensor_scalar(lat[:, 1:3, :], pr[:, C_QL:C_KVL].rearrange("p (k c) -> p k c", c=P),
                                        stat_inv[:, 10:11], None, ALU.mult)
                    v.tensor_tensor(lat[0:n, 0, :].rearrange("p (g c) -> p g c", c=HD),
                                    pr[:, C_K:C_V].rearrange("p (g c) -> p g c", c=HD),
                                    spread(stat_inv[0:n, 8:10], HD), ALU.mult)
                    v.tensor_scalar(lat[0:n, 3, :], pr[:, C_KVL:C_KR], stat_inv[0:n, 11:12], None, ALU.mult)\
                        .then_inc(lat_ready, 1)

                    H = MLA_HEADS
                    dve.wait_ge(job_out, place[s, "kv1"] + 1)
                    own = k_raw[0:n, :, 0:NOPE]
                    link(v.tensor_tensor(up_sq[0:n, :, 0:NOPE], own, own, ALU.mult))
                    link(v.tensor_reduce(head_stat[0:n, 0:H], up_sq[0:n, :, 0:NOPE], AX.X, ALU.add))
                    last = v.tensor_scalar(head_stat[0:n, 0:H], head_stat[0:n, 0:H], kr_sq[0:n, 0:1], 1.0 / QK,
                                           ALU.add, ALU.mult)
                    if s < MT:
                        dve.wait_ge(job_out, place[s, "q1"] + 1)
                        link(v.tensor_tensor(up_sq, q_raw[:], q_raw[:], ALU.mult))
                        link(v.tensor_reduce(head_stat[:, H:2 * H], up_sq, AX.X, ALU.add))
                        last = v.tensor_scalar(head_stat[:, H:2 * H], head_stat[:, H:2 * H], 1.0 / QK, None, ALU.mult)
                    last.then_inc(head_stat_ready, 1)
                    if s < MT:
                        rotate(q_rot, q_rot2, q_raw[:, :, NOPE:QK], repeat(cos_q[:, s, :], H),
                               repeat(sin_q[:, s, :], H))
                    dve.wait_ge(head_root_ready, s + 1)
                    link(v.reciprocal(head_inv[0:n, :], head_root[0:n, :]))
                    v.tensor_tensor(own, own, spread(head_inv[0:n, 0:H], NOPE), ALU.mult)
                    v.tensor_tensor(k_raw[0:n, :, NOPE:QK], repeat(k_rot[0:n, :], H),
                                    spread(head_inv[0:n, 0:H], ROPE), ALU.mult).then_inc(k_ready, 1)
                    if s < MT:
                        v.tensor_tensor(q_raw[:, :, 0:NOPE], q_raw[:, :, 0:NOPE],
                                        spread(head_inv[:, H:2 * H], NOPE), ALU.mult)
                        v.tensor_tensor(q_raw[:, :, NOPE:QK], q_rot, spread(head_inv[:, H:2 * H], ROPE),
                                        ALU.mult).then_inc(q_ready, 1)

            @block.tensor
            def _(pe):
                def start_job(t, name):
                    j = place[t, name]
                    if j >= 3:
                        pe.wait_ge(job_out, j - 2)
                    return job_bank[:, j % 3, :]

                def transposes(t, name, parts):
                    bank = start_job(t, name)
                    n = rows(t)
                    for i, part in parts:
                        w = part.shape[-1]
                        last = nc.tensor.transpose(bank[0:w, i * P:i * P + n], part, ident[0:n, 0:n])
                    last.then_inc(job_done, 1)

                def proj_part(t, part):
                    n = rows(t)
                    c0, c1 = PROJ[part]
                    if t >= 1:
                        pe.wait_ge(proj_out, 3 * (t - 1) + part + 1)
                    for k in range(DC):
                        last = nc.tensor.matmul(proj_bank[0:n, part, 0:c1 - c0], normT[:, t % 2, k, 0:n],
                                                w_in[:, k, c0:c1], start=(k == 0), stop=(k == DC - 1))
                    last.then_inc(proj_done, 1)

                for s in range(-1, MT + 1):
                    if s == -1:
                        pe.wait_ge(const_in, CONSTS)
                    if s + 1 <= MT:
                        t = s + 1
                        n = rows(t)
                        pe.wait_ge(x_normed, t + 1)
                        for b, freed in ((0, normT_lo), (1, normT_hi)):
                            if t >= 1:
                                pe.wait_ge(freed, t)
                            for k in range(4):
                                c = (4 * b + k) * P
                                last = nc.tensor.transpose(xT_bank[:, b, k * P:k * P + n],
                                                           xt[0:n, t % 3, c:c + P], ident[0:n, 0:n])
                            last.then_inc(xT_done, 1)
                    if s >= 0:
                        n = rows(s)
                        pe.wait_ge(lat_ready, s + 1)
                        if s < MT:
                            transposes(s, "qpairs", [(j, qn[:, j, :, :].rearrange("p g c -> p (g c)"))
                                                     for j in range(PAIRS)])
                        transposes(s, "lats", [(i, lat[0:n, i, :]) for i in ((0, 1, 2, 3) if s < MT else (0, 3))])
                    if s + 1 <= MT:
                        pe.wait_ge(normT_lo, s + 2)
                        pe.wait_ge(normT_hi, s + 2)
                        if s == -1:
                            pe.wait_ge(w_scaled, 1)
                        proj_part(s + 1, 0)
                    if s >= 0:
                        pe.wait_ge(job_out, place[s, "lats"] + 1)
                        for hf in range(2):
                            bank = start_job(s, f"kv{hf}")
                            nc.tensor.matmul(bank[0:n, :], latT[:, 2, 0:n], w_kvup[:, hf * 512:(hf + 1) * 512],
                                             start=True, stop=True).then_inc(job_done, 1)
                        for hf in range(2) if s < MT else ():
                            bank = start_job(s, f"q{hf}")
                            for k in range(2):
                                last = nc.tensor.matmul(bank[:, 0:4 * QK], latT[:, k, :],
                                                        w_qup[:, k, hf * 4 * QK:(hf + 1) * 4 * QK],
                                                        start=(k == 0), stop=(k == 1))
                            last.then_inc(job_done, 1)
                    if s + 1 <= MT:
                        proj_part(s + 1, 1)
                        proj_part(s + 1, 2)
                    if s >= 0:
                        pe.wait_ge(k_ready, s + 1)
                        for hf in range(2):
                            transposes(s, f"kT{hf}", [(i, k_raw[0:n, 4 * hf + i, :]) for i in range(4)])
                        if s < MT:
                            pe.wait_ge(q_ready, s + 1)
                            for hf in range(2):
                                transposes(s, f"qT{hf}", [(i, q_raw[:, 4 * hf + i, :]) for i in range(4)])


def window(t):
    return (P if t == 0 else 0), (BAND - P if t == TILES - 1 else BAND)


def attend(nc, io, keep):
    UNITS = MLA_HEADS + SWA_HEADS
    with ExitStack() as ctx:
        m = Mem(nc, ctx)
        w_out = m.sb("w_out_sb", [P, DC, D])
        band_bias = m.sb("band_bias", [P, SWA_HEADS, BAND])
        sink = m.sb("sink", [P, SWA_HEADS])
        no_rows = m.sb("no_rows", [HALF, 2 * D])
        v_meta = m.sb("v_meta", [P, MLA_HEADS, VD])
        resid = m.sb("resid", [P, 2, D])
        probs = m.sb("probs", [P, 2, SEQ])
        probsT = m.sb("probsT", [P, 2, DC, P])
        biased = m.sb("biased", [P, 2, BAND])
        meta_s = m.sb("meta_s", [P, 2, MLA_HEADS, META])
        meta_p = m.sb("meta_p", [P, MLA_HEADS * META])
        meta_pT = m.sb("meta_pT", [P, P])
        meta_max = m.sb("meta_max", [P, 2, MLA_HEADS])
        real_max = m.sb("real_max", [P, 2])
        neg_max = m.sb("neg_max", [P, 2])
        band_max = m.sb("band_max", [P, SWA_HEADS])
        neg_band = m.sb("neg_band", [P, SWA_HEADS])
        real_sum = m.sb("real_sum", [P, MLA_HEADS])
        meta_sum = m.sb("meta_sum", [P, MLA_HEADS])
        band_sum = m.sb("band_sum", [P, SWA_HEADS])
        sink_exp = m.sb("sink_exp", [P, SWA_HEADS])
        mla_inv = m.sb("mla_inv", [P, MLA_HEADS])
        swa_inv = m.sb("swa_inv", [P, SWA_HEADS])
        mixed = m.sb("mixed", [P, 2 * 512])
        mixedT = m.sb("mixedT", [P, DC, P])
        score_bank = m.ps("score_bank", [P, 2, 1024])
        act_bank = m.ps("act_bank", [P, 512])
        dve_bank = m.ps("dve_bank", [P, 512])
        mla_bank = m.ps("mla_bank", [P, 512])
        swa_bank = m.ps("swa_bank", [P, 512])
        swa_qT, swa_kT, swa_v = keep["swa_qT"], keep["swa_kT"], keep["swa_v"]
        mla_qT, mla_kT, mla_v = keep["mla_qT"], keep["mla_kT"], keep["mla_v"]
        ident = keep["ident"]

        const_in = m.sem("const_in_a")
        w_out_in = m.sem("w_out_in")
        v_meta_zero = m.sem("v_meta_zero")
        no_rows_set = m.sem("no_rows_set")
        y_zeroed = m.sem("y_zeroed")
        v_meta_in = m.sem("v_meta_in")
        resid_in = [m.sem(f"resid_in{i}") for i in range(2)]
        resid_out = [m.sem(f"resid_out{i}") for i in range(2)]
        scores_done = m.sem("scores_done")
        max_ready = m.sem("max_ready")
        band_ready = m.sem("band_ready")
        exp_done = m.sem("exp_done")
        meta_done = m.sem("meta_done")
        meta_read = m.sem("meta_read")
        act_T_done = m.sem("act_T_done")
        act_T_out = m.sem("act_T_out")
        dve_T_done = m.sem("dve_T_done")
        dve_T_out = m.sem("dve_T_out")
        values_done = m.sem("values_done")
        mla_done = m.sem("mla_done")
        mla_mixed = m.sem("mla_mixed")
        swa_mixed = m.sem("swa_mixed")
        sink_diff = m.sem("sink_diff")
        sink_done = m.sem("sink_done")
        attn_added = m.sem("attn_added")
        dve_own = m.sem("dve_own_a")

        fills, act_T, dve_T = [], [], []
        for n in range(TILES * UNITS + 8):
            t, i = divmod(n, UNITS)
            if t < TILES:
                fills.append(("unit", n))
            if 0 < n <= TILES * UNITS:
                mla = (n - 1) % UNITS < MLA_HEADS
                if mla:
                    act_T.append(("unit", n - 1))
                dve_T.append(("unit", n - 1))
            if i == 9 and t < TILES:
                act_T.append(("meta", t))
            if i == 3 and t >= 1:
                act_T.append(("mixed", t - 1))
                dve_T.append(("mixed", t - 1))
            if i == 5 and t >= 1:
                fills.append(("out", t - 1))
        at_fill = {x: j for j, x in enumerate(fills)}
        at_act = {x: j for j, x in enumerate(act_T)}
        at_dve = {x: j for j, x in enumerate(dve_T)}

        def band_units(n):
            t, i = divmod(n, UNITS)
            return t * SWA_HEADS + max(0, i + 1 - MLA_HEADS)

        def wait_fill_free(eng, j):
            if j < 2:
                return
            kind, n = fills[j - 2]
            if kind == "out":
                eng.wait_ge(attn_added, n + 1)
            elif n % UNITS < MLA_HEADS:
                eng.wait_ge(exp_done, n + 1)
            else:
                eng.wait_ge(band_ready, band_units(n))

        def band_parts(t):
            first, _ = window(t)
            parts = []
            if t > 0:
                parts.append((0 - first, (t - 1) * P, P, t - 1))
            parts.append((P - first, SEQ, META, MT))
            parts.append((P + META - first, t * P, P, t))
            if t < TILES - 1:
                parts.append((2 * P + META - first, (t + 1) * P, P, t + 1))
            whole = [x for x in parts if x[2] == P] + [x for x in parts if x[2] != P]
            return [(*x, j) for j, x in enumerate(whole)]

        with nc.Block() as block:

            @block.sync
            def _(sp):
                sp.dma_start(band_bias[:], io["band_bias"]).then_inc(const_in, 16)
                sp.dma_start(sink[:], io["swa_sink"][0].partition_broadcast(P)).then_inc(const_in, 16)
                sp.wait_ge(v_meta_zero, 1)
                for h in range(MLA_HEADS):
                    sp.dma_start(v_meta[h * META:(h + 1) * META, h, :], mla_v[0:META, MT, h, :]).then_inc(v_meta_in, 16)

                def load(t):
                    sp.dma_start(resid[:, t % 2, :], io["x"][0, t * P:(t + 1) * P, :]).then_inc(resid_in[t % 2], 16)

                load(0)
                load(1)
                sp.dma_start(w_out[:], io["w_out"][0].rearrange("(k p) n -> p k n", p=P)).then_inc(w_out_in, 16)
                for t in range(TILES):
                    sp.wait_ge(attn_added, t + 1)
                    sp.dma_start(io["h"][t * P:(t + 1) * P, :], resid[:, t % 2, :]).then_inc(resid_out[t % 2], 16)
                    if t + 2 < TILES:
                        sp.wait_ge(resid_out[t % 2], 16 * (t // 2 + 1))
                        load(t + 2)
                for b in range(2):
                    sp.wait_ge(resid_out[b], 16 * (TILES // 2))

            @block.gpsimd
            def _(pool):
                nc.gpsimd.memset(v_meta[:], 0.0).then_inc(v_meta_zero, 1)
                nc.gpsimd.memset(no_rows[:], 0.0).then_inc(no_rows_set, 1)
                pool.wait_ge(no_rows_set, 1)
                for b in range(LEAST, BLOCKS):
                    pool.dma_start(io["y"][b * SLOTS:(b + 1) * SLOTS, :].rearrange("(p j) d -> p (j d)", p=HALF),
                                   no_rows[:]).then_inc(y_zeroed, 16)
                pool.wait_ge(y_zeroed, 16 * (BLOCKS - LEAST))

            @block.scalar
            def _(act):
                def copy_T(key, out, src):
                    act.wait_ge(act_T_done, at_act[key] + 1)
                    nc.scalar.copy(out, src).then_inc(act_T_out, 1)

                for n in range(TILES * UNITS + 8):
                    t, i = divmod(n, UNITS)
                    u = n - 1
                    if 0 <= u < TILES * UNITS and u % UNITS < MLA_HEADS:
                        if u >= 2:
                            act.wait_ge(values_done, u - 1)
                        copy_T(("unit", u), probsT[:, u % 2, 0:4, :].rearrange("p k q -> p (k q)"), act_bank[:])
                    if i == 10 and t < TILES:
                        if t >= 1:
                            act.wait_ge(mla_done, t)
                        copy_T(("meta", t), meta_pT[:], act_bank[:, 0:P])
                    if i == 3 and t >= 1:
                        if t >= 2:
                            act.wait_ge(scores_done, at_fill["out", t - 2] + 1)
                        copy_T(("mixed", t - 1), mixedT[:, 0:4, :].rearrange("p k q -> p (k q)"), act_bank[:])
                    if i == 2 and t >= 1:
                        act.wait_ge(sink_diff, t)
                        nc.scalar.activation(sink_exp[:], sink_exp[:], ACT.Exp).then_inc(sink_done, 1)
                    if t >= TILES:
                        continue
                    j = at_fill["unit", n]
                    if n >= 2:
                        act.wait_ge(dve_T_done, at_dve["unit", n - 2] + 1)
                    if i < MLA_HEADS:
                        act.wait_ge(max_ready, t * MLA_HEADS + i + 1)
                        if i == 0 and t >= 1:
                            act.wait_ge(mla_mixed, t)
                        nc.scalar.activation(meta_p[:, i * META:(i + 1) * META], meta_s[:, t % 2, i, :], ACT.Exp,
                                             bias=neg_max[:, n % 2:n % 2 + 1], accum_out=meta_sum[:, i:i + 1])
                        nc.scalar.activation(probs[:, n % 2, :], score_bank[:, j % 2, :], ACT.Exp,
                                             bias=neg_max[:, n % 2:n % 2 + 1], accum_out=real_sum[:, i:i + 1])\
                            .then_inc(exp_done, 1)
                    else:
                        h = i - MLA_HEADS
                        w0, w1 = window(t)
                        act.wait_ge(band_ready, band_units(n))
                        if h == 0 and t >= 1:
                            act.wait_ge(swa_mixed, t)
                        nc.scalar.activation(probs[:, n % 2, 0:w1 - w0], biased[:, n % 2, 0:w1 - w0], ACT.Exp,
                                             bias=neg_band[:, h:h + 1], accum_out=band_sum[:, h:h + 1])\
                            .then_inc(exp_done, 1)

            @block.vector
            def _(dve):
                link = chain(dve, dve_own)
                v = nc.vector

                def take_meta(t):
                    if t >= 2:
                        dve.wait_ge(exp_done, (t - 2) * UNITS + MLA_HEADS)
                    dve.wait_ge(meta_done, t + 1)
                    v.tensor_copy(meta_s[:, t % 2, :, :].rearrange("p h c -> p (h c)"), swa_bank[:, 0:MLA_HEADS * META])
                    v.tensor_reduce(meta_max[:, t % 2, :],
                                    swa_bank[:, 0:MLA_HEADS * META].rearrange("p (h c) -> p h c", c=META),
                                    AX.X, ALU.max).then_inc(meta_read, 1)

                dve.wait_ge(const_in, 32)
                take_meta(0)
                for n in range(TILES * UNITS + 8):
                    t, i = divmod(n, UNITS)
                    if t < TILES:
                        j = at_fill["unit", n]
                        dve.wait_ge(scores_done, j + 1)
                        if i < MLA_HEADS:
                            if i == 0:
                                dve.wait_ge(meta_read, t + 1)
                            link(v.tensor_reduce(real_max[:, n % 2:n % 2 + 1], score_bank[:, j % 2, :], AX.X, ALU.max))
                            if n >= 2:
                                dve.wait_ge(exp_done, n - 1)
                            v.tensor_scalar(neg_max[:, n % 2:n % 2 + 1], real_max[:, n % 2:n % 2 + 1],
                                            meta_max[:, t % 2, i:i + 1], -1.0, ALU.max, ALU.mult).then_inc(max_ready, 1)
                        else:
                            h = i - MLA_HEADS
                            w0, w1 = window(t)
                            dve.wait_ge(exp_done, n - 1)
                            link(v.tensor_tensor_reduce(out=biased[:, n % 2, 0:w1 - w0],
                                                        in0=score_bank[:, j % 2, 0:w1 - w0],
                                                        in1=band_bias[:, h, w0:w1], scale=1.0,
                                                        scalar=sink[:, h:h + 1], op0=ALU.add, op1=ALU.max,
                                                        accum_out=band_max[:, h:h + 1]))
                            v.tensor_scalar(neg_band[:, h:h + 1], band_max[:, h:h + 1], -1.0, None, ALU.mult)\
                                .then_inc(band_ready, 1)
                    u = n - 1
                    if 0 <= u < TILES * UNITS:
                        if u >= 2:
                            dve.wait_ge(values_done, u - 1)
                        dve.wait_ge(dve_T_done, at_dve["unit", u] + 1)
                        if u % UNITS < MLA_HEADS:
                            last = v.tensor_copy(probsT[:, u % 2, 4:8, :].rearrange("p k q -> p (k q)"), dve_bank[:])
                        else:
                            k = len(band_parts(u // UNITS)) - 1
                            v.tensor_copy(probsT[:, u % 2, 0:k, :].rearrange("p k q -> p (k q)"), dve_bank[:, 0:k * P])
                            last = v.tensor_copy(probsT[0:META, u % 2, k, :], dve_bank[0:META, k * P:(k + 1) * P])
                        last.then_inc(dve_T_out, 1)
                    if i == 6 and t + 1 < TILES:
                        take_meta(t + 1)
                    if i == 11 and t < TILES:
                        dve.wait_ge(mla_done, t + 1)
                        dve.wait_ge(exp_done, t * UNITS + MLA_HEADS)
                        link(v.tensor_tensor(mla_inv[:], real_sum[:], meta_sum[:], ALU.add))
                        link(v.reciprocal(mla_inv[:], mla_inv[:]))
                        v.tensor_tensor(mixed[:, 512:1024].rearrange("p (h c) -> p h c", c=VD),
                                        mla_bank[:].rearrange("p (h c) -> p h c", c=VD),
                                        spread(mla_inv[:], VD), ALU.mult).then_inc(mla_mixed, 1)
                    if i == 1 and t >= 1:
                        dve.wait_ge(exp_done, t * UNITS)
                        v.tensor_tensor(sink_exp[:], sink[:], neg_band[:], ALU.add).then_inc(sink_diff, 1)
                    if i == 2 and t >= 1:
                        dve.wait_ge(sink_done, t)
                        dve.wait_ge(values_done, t * UNITS)
                        link(v.tensor_tensor(swa_inv[:], band_sum[:], sink_exp[:], ALU.add))
                        link(v.reciprocal(swa_inv[:], swa_inv[:]))
                        v.tensor_tensor(mixed[:, 0:512].rearrange("p (h c) -> p h c", c=HD),
                                        swa_bank[:].rearrange("p (h c) -> p h c", c=HD),
                                        spread(swa_inv[:], HD), ALU.mult).then_inc(swa_mixed, 1)
                    if i == 3 and t >= 1:
                        dve.wait_ge(dve_T_done, at_dve["mixed", t - 1] + 1)
                        if t >= 2:
                            dve.wait_ge(scores_done, at_fill["out", t - 2] + 1)
                        v.tensor_copy(mixedT[:, 4:8, :].rearrange("p k q -> p (k q)"), dve_bank[:]).then_inc(dve_T_out, 1)
                    if i == 6 and t >= 1:
                        j = at_fill["out", t - 1]
                        dve.wait_ge(resid_in[(t - 1) % 2], 16 * ((t - 1) // 2 + 1))
                        dve.wait_ge(scores_done, j + 1)
                        v.tensor_tensor(resid[:, (t - 1) % 2, :], resid[:, (t - 1) % 2, :], score_bank[:, j % 2, :],
                                        ALU.add).then_inc(attn_added, 1)

            @block.tensor
            def _(pe):
                def meta_scores(t):
                    if t >= 2:
                        pe.wait_ge(swa_mixed, t - 1)
                    for h in range(MLA_HEADS):
                        last = nc.tensor.matmul(swa_bank[:, h * META:(h + 1) * META], mla_qT[:, h, cols(t)],
                                                mla_kT[:, h, cols(MT)], start=True, stop=True)
                    last.then_inc(meta_done, 1)

                def scores(n):
                    t, i = divmod(n, UNITS)
                    j = at_fill["unit", n]
                    bank = score_bank[:, j % 2, :]
                    wait_fill_free(pe, j)
                    if i < MLA_HEADS:
                        for half in range(2):
                            last = nc.tensor.matmul(bank[:, half * 512:(half + 1) * 512], mla_qT[:, i, cols(t)],
                                                    mla_kT[:, i, half * 512:(half + 1) * 512], start=True, stop=True)
                    else:
                        g, pair = divmod(i - MLA_HEADS, PAIRS)
                        r = slice(g * HD, (g + 1) * HD)
                        for at, key, keys, _, _ in band_parts(t):
                            last = nc.tensor.matmul(bank[:, at:at + keys], swa_qT[r, pair, cols(t)],
                                                    swa_kT[r, key:key + keys], start=True, stop=True)
                    last.then_inc(scores_done, 1)

                def transpose_probs(n):
                    t, i = divmod(n, UNITS)
                    pe.wait_ge(exp_done, n + 1)
                    if i < MLA_HEADS:
                        if at_act["unit", n]:
                            pe.wait_ge(act_T_out, at_act["unit", n])
                        for k in range(4):
                            last = nc.tensor.transpose(act_bank[:, k * P:(k + 1) * P],
                                                       probs[:, n % 2, k * P:(k + 1) * P], ident[:])
                        last.then_inc(act_T_done, 1)
                    if at_dve["unit", n]:
                        pe.wait_ge(dve_T_out, at_dve["unit", n])
                    if i < MLA_HEADS:
                        for k in range(4):
                            last = nc.tensor.transpose(dve_bank[:, k * P:(k + 1) * P],
                                                       probs[:, n % 2, (4 + k) * P:(5 + k) * P], ident[:])
                    else:
                        for at, _, keys, _, slot in band_parts(t):
                            last = nc.tensor.transpose(dve_bank[0:keys, slot * P:(slot + 1) * P],
                                                       probs[:, n % 2, at:at + keys], ident[:])
                    last.then_inc(dve_T_done, 1)

                def values(n):
                    t, i = divmod(n, UNITS)
                    pe.wait_ge(dve_T_out, at_dve["unit", n] + 1)
                    if i < MLA_HEADS:
                        pe.wait_ge(act_T_out, at_act["unit", n] + 1)
                        if i == 0 and t >= 1:
                            pe.wait_ge(mla_mixed, t)
                        for k in range(DC):
                            last = nc.tensor.matmul(mla_bank[:, i * VD:(i + 1) * VD], probsT[:, n % 2, k, :],
                                                    mla_v[:, k, i, :], start=(i == 0 and k == 0), stop=False,
                                                    skip_group_check=True)
                    else:
                        h = i - MLA_HEADS
                        g = h // PAIRS
                        parts = band_parts(t)
                        if h == 0:
                            pe.wait_ge(meta_read, min(t + 2, TILES))
                        for x, (_, _, keys, kt, slot) in enumerate(parts):
                            last = nc.tensor.matmul(swa_bank[:, h * HD:(h + 1) * HD], probsT[0:keys, n % 2, slot, :],
                                                    swa_v[0:keys, kt, g * HD:(g + 1) * HD],
                                                    start=(x == 0), stop=(x == len(parts) - 1))
                    last.then_inc(values_done, 1)

                meta_scores(0)
                for n in range(TILES * UNITS + 8):
                    t, i = divmod(n, UNITS)
                    if i == 5 and t + 1 < TILES:
                        meta_scores(t + 1)
                    if t < TILES:
                        scores(n)
                    if 0 < n <= TILES * UNITS:
                        transpose_probs(n - 1)
                    if i == 9 and t < TILES:
                        pe.wait_ge(act_T_out, at_act["meta", t])
                        nc.tensor.transpose(act_bank[:, 0:P], meta_p[:], ident[:]).then_inc(act_T_done, 1)
                    if 1 < n <= TILES * UNITS + 1:
                        values(n - 2)
                    if i == 10 and t < TILES:
                        pe.wait_ge(act_T_out, at_act["meta", t] + 1)
                        if t == 0:
                            pe.wait_ge(v_meta_in, 16 * MLA_HEADS)
                        nc.tensor.matmul(mla_bank[:], meta_pT[:], v_meta[:].rearrange("p h c -> p (h c)"),
                                         start=False, stop=True, skip_group_check=True).then_inc(mla_done, 1)
                    if i == 3 and t >= 1:
                        pe.wait_ge(swa_mixed, t)
                        pe.wait_ge(mla_mixed, t)
                        for bank, out, done, key, c0 in ((act_bank, act_T_out, act_T_done, at_act["mixed", t - 1], 0),
                                                         (dve_bank, dve_T_out, dve_T_done, at_dve["mixed", t - 1], 4)):
                            pe.wait_ge(out, key)
                            for k in range(4):
                                c = (c0 + k) * P
                                last = nc.tensor.transpose(bank[:, k * P:(k + 1) * P], mixed[:, c:c + P], ident[:])
                            last.then_inc(done, 1)
                    if i == 5 and t >= 1:
                        j = at_fill["out", t - 1]
                        wait_fill_free(pe, j)
                        if t == 1:
                            pe.wait_ge(w_out_in, 16)
                        pe.wait_ge(act_T_out, at_act["mixed", t - 1] + 1)
                        pe.wait_ge(dve_T_out, at_dve["mixed", t - 1] + 1)
                        for half in range(2):
                            for k in range(DC):
                                last = nc.tensor.matmul(score_bank[:, j % 2, half * 512:(half + 1) * 512],
                                                        mixedT[:, k, :], w_out[:, k, half * 512:(half + 1) * 512],
                                                        start=(k == 0), stop=(k == DC - 1))
                        last.then_inc(scores_done, 1)


def route(nc, io, keep):
    with ExitStack() as ctx:
        m = Mem(nc, ctx)
        w_router = m.sb("w_router", [P, DC, E])
        b_router = m.sb("b_router", [P, E])
        g_ffn = m.sb("g_ffn", [P, D])
        tri = m.sb("tri", [P, P])
        ones = m.sb("ones", [P, P])
        expert_no = m.sb("expert_no", [P, E])
        block_no = m.sb("block_no", [P, BLOCKS + 1])
        token_no = m.sb("token_no", [P, TILES], I32)
        zeros = m.sb("zeros", [HALF, 2 * (BLOCKS + 1)], I32)
        ht = m.sb("ht", [P, 3, D])
        square = m.sb("square_r", [P, D])
        stat = m.sb("stat_r", [P, TILES, 3])
        normed = m.sb("normed_r", [P, 2, D])
        normT = m.sb("normT_r", [P, 2, DC, P])
        logits = m.sb("logits", [P, TILES, E])
        top = m.sb("top", [P, TILES, 8])
        top_i = m.sb("top_i", [P, TILES, 8], U32)
        top_f = m.sb("top_f", [P, TILES, TOPK])
        gate_sum = m.sb("gate_sum", [P, TILES])
        chosen = m.sb("chosen", [P, TOPK, TILES, E])
        sel = m.sb("sel", [P, TILES, E])
        before = m.sb("before", [P, TILES + 1, E])
        blocks = m.sb("blocks", [P, E])
        block_end = m.sb("block_end", [P, E])
        first_slot = m.sb("first_slot", [P, E])
        slot = m.sb("slot", [P, TILES, E])
        picked = m.sb("picked", [P, TOPK, TILES, E])
        slot_f = m.sb("slot_f", [P, TOPK, TILES])
        past = m.sb("past", [P, BLOCKS + 1, E])
        owner = m.sb("owner", [P, BLOCKS + 1])
        xT_bank = m.ps("xT_bank_r", [P, 2, 512])
        logit_bank = m.ps("logit_bank", [P, 2, 512])
        rank_bank = m.ps("rank_bank", [P, 512])
        count_bank = m.ps("count_bank", [P, 512])
        ident, gates, slot_i = keep["ident"], keep["gates"], keep["slot_i"]

        const_in = m.sem("const_in_r")
        h_in = [m.sem(f"h_in{i}") for i in range(3)]
        h_root = m.sem("h_root")
        h_normed = m.sem("h_normed")
        rows_out = [m.sem(f"rows_out{i}") for i in range(2)]
        xT_done = m.sem("xT_done_r")
        normT_lo = m.sem("normT_lo_r")
        normT_hi = m.sem("normT_hi_r")
        logits_done = m.sem("logits_done")
        logits_read = m.sem("logits_read")
        gate_diff = m.sem("gate_diff")
        gate_exp = m.sem("gate_exp")
        sel_ready = m.sem("sel_ready")
        ranked = m.sem("ranked")
        zeroed = m.sem("zeroed")
        table_zero = m.sem("table_zero")
        slots_ready = m.sem("slots_ready")
        scattered = m.sem("scattered")
        dve_own = m.sem("dve_own_r")

        consts = [
            (w_router[:], io["router_w"][0].rearrange("(k p) n -> p k n", p=P)),
            (b_router[:], io["router_b"][0].partition_broadcast(P)),
            (g_ffn[:], io["ffn_norm_g"][0].partition_broadcast(P)),
            (tri[:], io["tri"]), (expert_no[:], io["expert_no"]),
            (block_no[:], io["block_no"]), (token_no[:], io["token_no"]),
        ]

        with nc.Block() as block:

            @block.sync
            def _(sp):
                for t in range(TILES):
                    if t >= 3:
                        sp.wait_ge(h_normed, t - 2)
                    sp.dma_start(ht[:, t % 3, :], io["h"][t * P:(t + 1) * P, :]).then_inc(h_in[t % 3], 16)
                    if t >= 1:
                        sp.wait_ge(h_normed, t)
                        sp.dma_start(io["rows"][(t - 1) * P:t * P, :], normed[:, (t - 1) % 2, :])\
                            .then_inc(rows_out[(t - 1) % 2], 16)
                t = TILES
                sp.wait_ge(h_normed, t)
                sp.dma_start(io["rows"][(t - 1) * P:t * P, :], normed[:, (t - 1) % 2, :])\
                    .then_inc(rows_out[(t - 1) % 2], 16)
                for b in range(2):
                    sp.wait_ge(rows_out[b], 16 * (TILES // 2))

            @block.gpsimd
            def _(pool):
                nc.gpsimd.memset(zeros[:], 0).then_inc(zeroed, 1)
                pool.wait_ge(zeroed, 1)
                pool.dma_start(io["slot_token"].rearrange("(p c) one -> p (c one)", p=HALF), zeros[:])\
                    .then_inc(table_zero, 16)
                pool.wait_ge(table_zero, 16)
                pool.wait_ge(slots_ready, 1)
                for t in range(TILES):
                    for k in range(TOPK):
                        pool.indirect_dma_start(
                            out=io["slot_token"], out_offset=bass.IndirectOffsetOnAxis(ap=slot_i[:, k, t:t + 1], axis=0),
                            in_=token_no[:, t:t + 1], in_offset=None,
                            bounds_check=BLOCKS * SLOTS - 1, oob_is_err=False).then_inc(scattered, 16)
                pool.wait_ge(scattered, 16 * TILES * TOPK)

            @block.scalar
            def _(act):
                for dst, src in consts:
                    act.dma_start(dst, src).then_inc(const_in, 16)
                own = 0
                for t in range(TILES):
                    act.wait_ge(h_in[t % 3], 16 * (t // 3 + 1))
                    nc.scalar.activation(square[:], ht[:, t % 3, :], ACT.Square, accum_out=stat[:, t, 0:1])\
                        .then_inc(keep["act_own"], 1)
                    own += 1
                    act.wait_ge(keep["act_own"], own)
                    nc.scalar.activation(stat[:, t, 1:2], stat[:, t, 0:1], ACT.Sqrt, scale=1.0 / D,
                                         bias=keep["eps"][:]).then_inc(h_root, 1)
                    if t >= 1:
                        act.wait_ge(xT_done, 2 * t - 1)
                        if t >= 3:
                            act.wait_ge(logits_done, t - 2)
                        nc.scalar.copy(normT[:, (t - 1) % 2, 0:4, :].rearrange("p k q -> p (k q)"), xT_bank[:, 0, :])\
                            .then_inc(normT_lo, 1)
                act.wait_ge(xT_done, 2 * TILES - 1)
                act.wait_ge(logits_done, TILES - 2)
                nc.scalar.copy(normT[:, (TILES - 1) % 2, 0:4, :].rearrange("p k q -> p (k q)"), xT_bank[:, 0, :])\
                    .then_inc(normT_lo, 1)
                act.wait_ge(gate_diff, 1)
                nc.scalar.activation(gates[:], gates[:], ACT.Exp).then_inc(gate_exp, 1)

            @block.vector
            def _(dve):
                link = chain(dve, dve_own)
                v = nc.vector

                def norm(t):
                    dve.wait_ge(h_root, t + 1)
                    link(v.reciprocal(stat[:, t, 2:3], stat[:, t, 1:2]))
                    if t >= 2:
                        dve.wait_ge(xT_done, 2 * (t - 1))
                        dve.wait_ge(rows_out[t % 2], 16 * (t // 2))
                    v.scalar_tensor_tensor(normed[:, t % 2, :], ht[:, t % 3, :], stat[:, t, 2:3], g_ffn[:],
                                           ALU.mult, ALU.mult).then_inc(h_normed, 1)

                def take_logits(t):
                    dve.wait_ge(logits_done, t + 1)
                    own = v.tensor_tensor(logits[:, t, :], logit_bank[:, t % 2, 0:E], b_router[:], ALU.add)
                    own.then_inc(logits_read, 1)
                    dve.wait_ge(logits_read, t + 1)
                    link(v.max(out=top[:, t, :], in_=logits[:, t, :]))
                    link(v.max_index(out=top_i[:, t, :], in_max=top[:, t, :], in_values=logits[:, t, :]))

                dve.wait_ge(const_in, 16 * len(consts))
                v.memset(ones[:], 1.0)
                v.memset(before[:, 0, :], 0.0)
                for t in range(TILES + 1):
                    if t < TILES:
                        norm(t)
                    if t >= 1:
                        dve.wait_ge(xT_done, 2 * t)
                        if t >= 3:
                            dve.wait_ge(logits_done, t - 2)
                        v.tensor_copy(normT[:, (t - 1) % 2, 4:8, :].rearrange("p k q -> p (k q)"), xT_bank[:, 1, :])\
                            .then_inc(normT_hi, 1)
                    if t >= 2:
                        take_logits(t - 2)
                take_logits(TILES - 1)

                link(v.tensor_copy(top_f[:], top_i[:, :, 0:TOPK]))
                v.tensor_tensor(gates[:], top[:, :, 0:TOPK],
                                top[:, :, 0:1].to_broadcast([P, TILES, TOPK]), ALU.subtract).then_inc(gate_diff, 1)
                for k in range(TOPK):
                    last = v.tensor_tensor(chosen[:, k], repeat(expert_no[:], TILES), spread(top_f[:, :, k], E),
                                           ALU.is_equal)
                link(last)
                v.tensor_tensor(sel[:], chosen[:, 0], chosen[:, 1], ALU.add)
                link(v.tensor_tensor(picked[:, 0], chosen[:, 2], chosen[:, 3], ALU.add))
                link(v.tensor_tensor(sel[:], sel[:], picked[:, 0], ALU.add))
                for t in range(TILES):
                    last = v.tensor_tensor(before[:, t + 1, :], before[:, t, :], sel[:, t, :], ALU.add)
                    if t < TILES - 1:
                        link(last)
                last.then_inc(sel_ready, 1)
                dve.wait_ge(gate_exp, 1)
                link(v.tensor_reduce(gate_sum[:], gates[:], AX.X, ALU.add))
                link(v.reciprocal(gate_sum[:], gate_sum[:]))
                link(v.tensor_tensor(gates[:], gates[:], spread(gate_sum[:], TOPK), ALU.mult))

                dve.wait_ge(ranked, 1)
                link(v.tensor_scalar(blocks[:], count_bank[:, 0:E], 0.0, None, ALU.is_gt))
                for r in range(1, ROUNDS):
                    link(v.scalar_tensor_tensor(blocks[:], count_bank[:, 0:E], float(r * SLOTS), blocks[:],
                                                ALU.is_gt, ALU.add))
                link(v.tensor_tensor_scan(block_end[:], ones[:, 0:E], blocks[:], 0.0, ALU.mult, ALU.add))
                link(v.tensor_tensor(first_slot[:], block_end[:], blocks[:], ALU.subtract))
                link(v.tensor_scalar(first_slot[:], first_slot[:], float(SLOTS), None, ALU.mult))
                link(v.tensor_tensor(slot[:], rank_bank[:, 0:TILES * E].rearrange("p (t e) -> p t e", e=E),
                                     repeat(first_slot[:], TILES), ALU.add))
                for k in range(TOPK):
                    last = v.tensor_tensor(picked[:, k], chosen[:, k], slot[:], ALU.mult)
                link(last)
                for k in range(TOPK):
                    last = v.tensor_reduce(slot_f[:, k, :], picked[:, k], AX.X, ALU.add)
                link(last)
                v.tensor_copy(slot_i[:], slot_f[:]).then_inc(slots_ready, 1)
                link(v.tensor_tensor(past[:], repeat(block_end[:], BLOCKS + 1), spread(block_no[:], E), ALU.is_le))
                link(v.tensor_reduce(owner[:], past[:], AX.X, ALU.add))
                v.tensor_scalar(keep["owner_i"][:], owner[:], float(E - 1), None, ALU.min)
                link(v.tensor_copy(keep["blocks_i"][:], block_end[:, E - 1:E]))

            @block.tensor
            def _(pe):
                pe.wait_ge(const_in, 16 * len(consts))
                for t in range(TILES + 1):
                    if t < TILES:
                        pe.wait_ge(h_normed, t + 1)
                        for b, freed in ((0, normT_lo), (1, normT_hi)):
                            if t >= 1:
                                pe.wait_ge(freed, t)
                            for k in range(4):
                                c = (4 * b + k) * P
                                last = nc.tensor.transpose(xT_bank[:, b, k * P:(k + 1) * P],
                                                           normed[:, t % 2, c:c + P], ident[:])
                            last.then_inc(xT_done, 1)
                    if t >= 1:
                        pe.wait_ge(normT_lo, t)
                        pe.wait_ge(normT_hi, t)
                        if t >= 3:
                            pe.wait_ge(logits_read, t - 2)
                        for k in range(DC):
                            last = nc.tensor.matmul(logit_bank[:, (t - 1) % 2, 0:E], normT[:, (t - 1) % 2, k, :],
                                                    w_router[:, k, :], start=(k == 0), stop=(k == DC - 1))
                        last.then_inc(logits_done, 1)
                pe.wait_ge(sel_ready, 1)
                nc.tensor.matmul(rank_bank[:, 0:TILES * E], tri[:], sel[:].rearrange("p t e -> p (t e)"),
                                 start=True, stop=False)
                nc.tensor.matmul(rank_bank[:, 0:TILES * E], ones[:], before[:, 0:TILES, :].rearrange("p t e -> p (t e)"),
                                 start=False, stop=True)
                nc.tensor.matmul(count_bank[:, 0:E], ones[:], before[:, TILES, :], start=True, stop=True)\
                    .then_inc(ranked, 1)


def experts(nc, io, keep):
    with ExitStack() as ctx:
        m = Mem(nc, ctx)
        HF = FF // 2
        w_gate = m.sb("w_gate_sb", [P, 2, DC, HF])
        w_up = m.sb("w_up_sb", [P, 2, DC, HF])
        w_down = m.sb("w_down_sb", [P, 2, FC, D // 2])
        bias_rows = m.sb("bias_rows", [3 * FC, P])
        bias_gu = m.sb("bias_gu", [P, 2 * FC])
        bias_next = m.sb("bias_next", [P, FC])
        bias_down = m.sb("bias_down", [P, FC])
        slot_rows = m.sb("slot_rows", [HALF, 2], U32)
        x_rows = m.sb("x_rows", [HALF, 2, D])
        xT = m.sb("xT", [P, DC, SLOTS])
        g_in = m.sb("g_in", [P, 2, SLOTS])
        u_in = m.sb("u_in", [P, 2, SLOTS])
        sig = m.sb("sig", [P, 2, SLOTS])
        g_sig = m.sb("g_sig", [P, 2, SLOTS])
        hidden = m.sb("hidden", [P, FC, SLOTS])
        yT = m.sb("yT", [P, DC, SLOTS])
        y_rows = m.sb("y_rows", [HALF, 2, D])
        spare = m.sb("spare", [P, 8])
        g_bank = m.ps("g_bank", [P, 2, 512])
        u_bank = m.ps("u_bank", [P, 2, 512])
        act_bank = m.ps("act_bank_e", [P, 512])
        dve_bank = m.ps("dve_bank_e", [P, 512])
        down_bank = m.ps("down_bank", [P, 2, 512])
        ident = keep["ident"]

        gate_in = [m.sem(f"gate_in{i}") for i in range(2)]
        up_in = [m.sem(f"up_in{i}") for i in range(2)]
        down_in = [m.sem(f"down_in{i}") for i in range(2)]
        bias_in = m.sem("bias_in")
        slots_in = m.sem("slots_in")
        slots_seen = m.sem("slots_seen")
        spare_set = m.sem("spare_set")
        x_in = m.sem("x_in_e")
        x_done = [m.sem(f"x_done{i}") for i in range(2)]
        x_out = [m.sem(f"x_out{i}") for i in range(2)]
        y_done = [m.sem(f"y_done{i}") for i in range(2)]
        y_out = [m.sem(f"y_out{i}") for i in range(2)]
        gu_done = m.sem("gu_done")
        gu_read = m.sem("gu_read")
        g_ready = m.sem("g_ready")
        sig_ready = m.sem("sig_ready")
        g_sig_ready = m.sem("g_sig_ready")
        hidden_ready = m.sem("hidden_ready")
        down_done = m.sem("down_done")
        down_read = m.sem("down_read")
        bias_set = m.sem("bias_set")
        y_stored = m.sem("y_stored")

        with nc.Block() as block:

            @block.sync
            def _(sp):
                def expert_of(b):
                    return sp.value_load(keep["owner_i"][0:1, bass.ds(b, 1)], min_val=0, max_val=E - 1)

                def load_biases(e):
                    for i, name in enumerate(("b_gate", "b_up", "b_down")):
                        sp.dma_start(bias_rows[i * FC:(i + 1) * FC, :],
                                     io[name][bass.ds(e, 1), :].rearrange("one (f p) -> (one f) p", p=P))\
                            .then_inc(bias_in, 16)

                def load(e, b=None):
                    for half in range(2):
                        c = slice(half * HF, (half + 1) * HF)
                        if b is not None:
                            sp.wait_ge(gu_done, b * FC + 4 * (half + 1))
                        for w, name, arrived in ((w_gate, "w_gate", gate_in), (w_up, "w_up", up_in)):
                            sp.dma_start(w[:, half], io[name][bass.ds(e, 1), :, c]
                                         .rearrange("one (k p) n -> p (one k) n", p=P)).then_inc(arrived[half], 16)
                    for half in range(2):
                        c = slice(half * HF, (half + 1) * HF)
                        if b is not None:
                            sp.wait_ge(down_done, b * DC + 4 * (half + 1))
                        sp.dma_start(w_down[:, half], io["w_down"][bass.ds(e, 1), :, c]
                                     .rearrange("one (k p) n -> p (one k) n", p=P)).then_inc(down_in[half], 16)

                count = sp.value_load(keep["blocks_i"][0:1, 0:1], min_val=1, max_val=BLOCKS)
                first = expert_of(0)
                load_biases(first)
                load(first)
                with sp.Fori(0, BLOCKS) as b:
                    e = expert_of(b + 1)
                    with sp.If(b < count):
                        sp.wait_ge(x_done[1], b * 2 + 2)
                        load_biases(e)
                    with sp.If(b + 1 < count):
                        load(e, b)

            @block.gpsimd
            def _(pool):
                def gather(b):
                    pool.dma_start(slot_rows[:], io["slot_token_u"][bass.ds(b * SLOTS, SLOTS), :]
                                   .rearrange("(p j) one -> p (j one)", p=HALF)).then_inc(slots_in, 16)
                    pool.wait_ge(slots_in, b * 16 + 16)
                    nc.gpsimd.tensor_tensor(spare[:, 4:5], spare[:, 3:4], spare[:, 3:4], ALU.add)\
                        .then_inc(slots_seen, 1)
                    for j in range(2):
                        pool.indirect_dma_start(
                            out=x_rows[:, j, :], out_offset=None, in_=io["rows"],
                            in_offset=bass.IndirectOffsetOnAxis(ap=slot_rows[:, j:j + 1], axis=0),
                            bounds_check=last_token, oob_is_err=False).then_inc(x_in, 16)

                count = pool.value_load(keep["blocks_i"][0:1, 0:1], min_val=1, max_val=BLOCKS)
                last_token = pool.to_reg(SEQ - 1)
                nc.gpsimd.memset(spare[:, 3:4], 0.0).then_inc(spare_set, 1)
                pool.wait_ge(spare_set, 1)
                pool.dma_start(spare[0:1, 7:8], io["ident"][0:1, 0:1]).then_inc(y_stored, 16)
                gather(0)
                with pool.Fori(0, BLOCKS) as b:
                    with pool.If(b < count):
                        pool.wait_ge(slots_seen, b + 1)
                        pool.wait_ge(x_done[1], b * 2 + 2)
                        gather(b + 1)
                        for out in y_out:
                            pool.wait_ge(out, b * 2 + 4)
                        pool.dma_start(io["y"][bass.ds(b * SLOTS, SLOTS), :].rearrange("(p j) d -> p j d", p=HALF),
                                       y_rows[:]).then_inc(y_stored, 16)
                pool.wait_ge(y_stored, count * 16 + 16)

            @block.scalar
            def _(act):
                count = act.value_load(keep["blocks_i"][0:1, 0:1], min_val=1, max_val=BLOCKS)

                def x_copies(b):
                    for i in range(2):
                        act.wait_ge(x_done[0], b * 2 + (i + 1))
                        nc.scalar.copy(xT[:, 4 * i:4 * i + 2, :].rearrange("p k q -> p (k q)"),
                                       act_bank[:, 0:2 * SLOTS]).then_inc(x_out[0], 1)

                nc.scalar.copy(spare[:, 1:2], ident[:, 0:1]).then_inc(down_read, 2)
                nc.scalar.copy(spare[:, 0:1], ident[:, 0:1]).then_inc(y_out[0], 2)
                x_copies(0)
                with act.Fori(0, BLOCKS) as b:
                    with act.If(b < count):
                        for f in range(FC):
                            act.wait_ge(g_ready, b * FC + (f + 1))
                            nc.scalar.activation(sig[:, f % 2, :], g_in[:, f % 2, :], ACT.Sigmoid, scale=ALPHA)\
                                .then_inc(sig_ready, 1)
                        x_copies(b + 1)
                        act.wait_ge(bias_set, b + 1)
                        for c in range(DC):
                            act.wait_ge(down_done, b * DC + (c + 1))
                            nc.scalar.activation(yT[:, c, :], down_bank[:, c % 2, 0:SLOTS], ACT.Identity,
                                                 bias=bias_down[:, c:c + 1]).then_inc(down_read, 1)
                        act.wait_ge(y_stored, b * 16 + 16)
                        for half in range(2):
                            act.wait_ge(y_done[0], b * 2 + (half + 1))
                            nc.scalar.copy(y_rows[:, 0, half * 512:(half + 1) * 512], act_bank[0:HALF, :])\
                                .then_inc(y_out[0], 1)

            @block.vector
            def _(dve):
                v = nc.vector
                count = dve.value_load(keep["blocks_i"][0:1, 0:1], min_val=1, max_val=BLOCKS)

                def x_copies(b):
                    for i in range(2):
                        dve.wait_ge(x_done[1], b * 2 + (i + 1))
                        if i == 0:
                            at = 2 * SLOTS
                            v.tensor_copy(bias_gu[:, 0:FC], dve_bank[:, at:at + FC])
                            v.tensor_scalar(bias_gu[:, FC:2 * FC], dve_bank[:, at + FC:at + 2 * FC], 1.0, None, ALU.add)
                            v.tensor_copy(bias_next[:], dve_bank[:, at + 2 * FC:at + 3 * FC])
                        v.tensor_copy(xT[:, 4 * i + 2:4 * i + 4, :].rearrange("p k q -> p (k q)"),
                                      dve_bank[:, 0:2 * SLOTS]).then_inc(x_out[1], 1)

                v.memset(spare[:, 2:3], 0.0).then_inc(gu_read, 2)
                v.memset(spare[:, 5:6], 0.0).then_inc(y_out[1], 2)
                x_copies(0)
                with dve.Fori(0, BLOCKS) as b:
                    with dve.If(b < count):
                        dve.wait_ge(x_out[1], b * 2 + 2)
                        dve.wait_ge(down_read, b * DC + 2)
                        v.tensor_copy(bias_down[:], bias_next[:]).then_inc(bias_set, 1)
                        for f in range(FC + 1):
                            if f < FC:
                                dve.wait_ge(gu_done, b * FC + (f + 1))
                                if f >= 2:
                                    dve.wait_ge(hidden_ready, b * FC + (f - 1))
                                v.tensor_scalar(g_in[:, f % 2, :], g_bank[:, f % 2, 0:SLOTS], bias_gu[:, f:f + 1],
                                                LIMIT, ALU.add, ALU.min).then_inc(g_ready, 1)
                                v.tensor_scalar(u_in[:, f % 2, :], u_bank[:, f % 2, 0:SLOTS],
                                                bias_gu[:, FC + f:FC + f + 1], 1.0 + LIMIT, ALU.add, ALU.min)\
                                    .then_inc(gu_read, 1)
                            if f >= 1:
                                s = f - 1
                                dve.wait_ge(sig_ready, b * FC + f)
                                v.tensor_tensor(g_sig[:, s % 2, :], g_in[:, s % 2, :], sig[:, s % 2, :], ALU.mult)\
                                    .then_inc(g_sig_ready, 1)
                                dve.wait_ge(g_sig_ready, b * FC + f)
                                v.scalar_tensor_tensor(hidden[:, s, :], u_in[:, s % 2, :], 1.0 - LIMIT, g_sig[:, s % 2, :],
                                                       ALU.max, ALU.mult).then_inc(hidden_ready, 1)
                        x_copies(b + 1)
                        dve.wait_ge(y_stored, b * 16 + 16)
                        for half in range(2):
                            dve.wait_ge(y_done[1], b * 2 + (half + 1))
                            v.tensor_copy(y_rows[:, 1, half * 512:(half + 1) * 512], dve_bank[0:HALF, :])\
                                .then_inc(y_out[1], 1)

            @block.tensor
            def _(pe):
                banks = (act_bank, dve_bank)
                count = pe.value_load(keep["blocks_i"][0:1, 0:1], min_val=1, max_val=BLOCKS)

                def transpose_x(b, last_b):
                    pe.wait_ge(x_in, b * 32 + 32)
                    pe.wait_ge(bias_in, b * 48 + 48)
                    for x in range(4):
                        bank = banks[x % 2]
                        if x >= 2:
                            pe.wait_ge(x_out[x % 2], b * 2 + 1)
                        elif last_b is not None:
                            pe.wait_ge(y_out[x % 2], last_b * 2 + 2)
                        for c in range(2):
                            for j in range(2):
                                at, k = (2 * c + j) * HALF, 2 * x + c
                                last = nc.tensor.transpose(bank[:, at:at + HALF], x_rows[:, j, k * P:(k + 1) * P],
                                                           ident[0:HALF, 0:HALF])
                        if x == 1:
                            at = 2 * SLOTS
                            last = nc.tensor.transpose(bank[:, at:at + 3 * FC], bias_rows[:],
                                                       ident[0:3 * FC, 0:3 * FC])
                        last.then_inc(x_done[x % 2], 1)

                def transpose_y(b, half):
                    pe.wait_ge(down_read, b * DC + (4 * half + 6))
                    for j, bank in enumerate(banks):
                        if half == 0:
                            pe.wait_ge(x_out[j], b * 2 + 4)
                        else:
                            pe.wait_ge(y_out[j], b * 2 + 3)
                        for k in range(4):
                            last = nc.tensor.transpose(bank[0:HALF, k * P:(k + 1) * P],
                                                       yT[:, 4 * half + k, j * HALF:(j + 1) * HALF], ident[:])
                        last.then_inc(y_done[j], 1)

                transpose_x(0, None)
                with pe.Fori(0, BLOCKS) as b:
                    with pe.If(b < count):
                        for out in x_out:
                            pe.wait_ge(out, b * 2 + 2)
                        for f in range(FC):
                            half, c = divmod(f, FC // 2)
                            if c == 0:
                                pe.wait_ge(gate_in[half], b * 16 + 16)
                                pe.wait_ge(up_in[half], b * 16 + 16)
                            pe.wait_ge(gu_read, b * FC + (f + 1))
                            for w, bank in ((w_gate, g_bank), (w_up, u_bank)):
                                for k in range(DC):
                                    last = nc.tensor.matmul(bank[:, f % 2, 0:SLOTS],
                                                            w[:, half, k, c * P:(c + 1) * P], xT[:, k, :],
                                                            start=(k == 0), stop=(k == DC - 1))
                            last.then_inc(gu_done, 1)
                        transpose_x(b + 1, b)
                        pe.wait_ge(hidden_ready, b * FC + FC)
                        for c in range(DC):
                            half, c4 = divmod(c, DC // 2)
                            if c4 == 0:
                                pe.wait_ge(down_in[half], b * 16 + 16)
                            pe.wait_ge(down_read, b * DC + (c + 1))
                            for k in range(FC):
                                last = nc.tensor.matmul(down_bank[:, c % 2, 0:SLOTS],
                                                        w_down[:, half, k, c4 * P:(c4 + 1) * P], hidden[:, k, :],
                                                        start=(k == 0), stop=(k == FC - 1))
                            last.then_inc(down_done, 1)
                            if c == 5:
                                transpose_y(b, 0)
                        transpose_y(b, 1)


def combine(nc, io, keep):
    with ExitStack() as ctx:
        m = Mem(nc, ctx)
        picked = m.sb("picked_c", [P, 3, TOPK, D])
        acc = m.sb("acc", [P, 3, D])
        rows_in = [m.sem(f"rows_in{i}") for i in range(3)]
        acc_in = [m.sem(f"acc_in{i}") for i in range(3)]
        added = m.sem("added")
        summed = m.sem("summed")
        out_stored = [m.sem(f"out_stored{i}") for i in range(3)]

        with nc.Block() as block:

            @block.sync
            def _(sp):
                for t in range(TILES + 1):
                    if t < TILES:
                        if t >= 3:
                            sp.wait_ge(out_stored[t % 3], 16 * (t // 3))
                        sp.dma_start(acc[:, t % 3, :], io["h"][t * P:(t + 1) * P, :]).then_inc(acc_in[t % 3], 16)
                    if t >= 1:
                        sp.wait_ge(summed, t)
                        sp.dma_start(io["out"][0, (t - 1) * P:t * P, :], acc[:, (t - 1) % 3, :])\
                            .then_inc(out_stored[(t - 1) % 3], 16)
                for b in range(3):
                    sp.wait_ge(out_stored[b], 16 * len(range(b, TILES, 3)))

            @block.gpsimd
            def _(pool):
                for t in range(TILES):
                    if t >= 3:
                        pool.wait_ge(summed, t - 2)
                    for k in range(TOPK):
                        pool.indirect_dma_start(
                            out=picked[:, t % 3, k, :], out_offset=None, in_=io["y"],
                            in_offset=bass.IndirectOffsetOnAxis(ap=keep["slot_i"][:, k, t:t + 1], axis=0),
                            bounds_check=BLOCKS * SLOTS - 1, oob_is_err=False).then_inc(rows_in[t % 3], 16)

            @block.vector
            def _(dve):
                for t in range(TILES):
                    dve.wait_ge(acc_in[t % 3], 16 * (t // 3 + 1))
                    dve.wait_ge(rows_in[t % 3], 16 * TOPK * (t // 3 + 1))
                    for k in range(TOPK):
                        if k:
                            dve.wait_ge(added, (TOPK - 1) * t + k)
                        nc.vector.scalar_tensor_tensor(acc[:, t % 3, :], picked[:, t % 3, k, :],
                                                       keep["gates"][:, t, k:k + 1], acc[:, t % 3, :],
                                                       ALU.mult, ALU.add).then_inc(added if k < TOPK - 1 else summed, 1)


def program(nc, io):
    with ExitStack() as ctx:
        m = Mem(nc, ctx)
        keep = {
            "ident": m.sb("ident_sb", [P, P]),
            "eps": m.sb("eps", [P, 1]),
            "gates": m.sb("gates", [P, TILES, TOPK]),
            "slot_i": m.sb("slot_i", [P, TOPK, TILES], U32),
            "owner_i": m.sb("owner_i", [P, BLOCKS + 1], I32),
            "blocks_i": m.sb("blocks_i", [P, 1], I32),
            "act_own": m.sem("act_own_r"),
        }
        with nc.Block() as block:

            @block.vector
            def _(dve):
                nc.vector.memset(keep["eps"][:], EPS)

        with ExitStack() as attention:
            m = Mem(nc, attention)
            keep["swa_qT"] = m.sb("swa_qT", [P, PAIRS, SEQ])
            keep["swa_kT"] = m.sb("swa_kT", [P, KEYS])
            keep["swa_v"] = m.sb("swa_v", [P, MT + 1, SWA_KV * HD])
            keep["mla_qT"] = m.sb("mla_qT", [QK, MLA_HEADS, SEQ])
            keep["mla_kT"] = m.sb("mla_kT", [QK, MLA_HEADS, KEYS])
            keep["mla_v"] = m.sb("mla_v", [P, MT + 1, MLA_HEADS, VD])
            project(nc, io, keep)
            attend(nc, io, keep)
        route(nc, io, keep)
        experts(nc, io, keep)
        combine(nc, io, keep)


def constants():
    import numpy as np

    f = np.float32
    row, col = np.arange(P)[:, None], np.arange(P)[None, :]
    pos = np.zeros((P, MT + 1), f)
    for t in range(TILES):
        pos[:, t] = META + t * P + np.arange(P)
    pos[:META, MT] = np.arange(META)
    half = ROPE // 2
    inv = (1.0 / (f(10000.0) ** (np.arange(half, dtype=f) / f(half)))).astype(f)
    angle = (pos[:, :, None] * inv).astype(f)
    cos, sin = np.cos(angle).astype(f), np.sin(angle).astype(f)
    band = np.empty((P, SWA_HEADS, BAND), f)
    for h in range(SWA_HEADS):
        slope = f(2.0 ** (-8.0 * (h + 1) / SWA_HEADS))
        for c0, shift in ((0, -P), (P + META, 0), (2 * P + META, P)):
            dist = np.abs(row - (col + shift))
            band[:, h, c0:c0 + P] = np.where(dist <= P, -slope * dist.astype(f), f(-1e30))
        band[:, h, P:P + META] = 0.0
    inv_n = np.array([1 / HD] * 10 + [1 / Q_LORA, 1 / KV_LORA], f)
    return {
        "ident": np.eye(P, dtype=f),
        "tri": (row < col).astype(f),
        "cos2": np.concatenate([cos, cos], 2),
        "sin2": np.concatenate([-sin, sin], 2),
        "band_bias": band,
        "inv_n": np.tile(inv_n, (P, 1)),
        "expert_no": np.tile(np.arange(E, dtype=f), (P, 1)),
        "block_no": np.tile(np.arange(BLOCKS + 1, dtype=f), (P, 1)),
        "token_no": (np.arange(TILES)[None, :] * P + np.arange(P)[:, None]).astype(np.int32),
    }


def kernel(**inputs):
    import numpy as np
    import concourse.bacc as bacc
    from concourse.bass_utils import run_bass_kernel_spmd

    nc = bacc.Bacc("TRN2", target_bir_lowering=False, num_devices=1)
    arrays, io = {}, {}
    for name, a in {**inputs, **constants()}.items():
        a = np.ascontiguousarray(a)
        if name in ("w_gate", "w_up", "w_down", "b_gate", "b_up", "b_down"):
            a = a[0]
        arrays["in_" + name] = a
        io[name] = nc.dram_tensor("in_" + name, a.shape, mybir.dt.from_np(a.dtype), kind="ExternalInput").ap()
    io["out"] = nc.dram_tensor("out_y", (1, SEQ, D), F32, kind="ExternalOutput").ap()
    io["h"] = nc.dram_tensor("residual", (SEQ, D), F32).ap()
    io["rows"] = nc.dram_tensor("ffn_rows", (SEQ, D), F32).ap()
    io["y"] = nc.dram_tensor("expert_rows", (BLOCKS * SLOTS, D), F32).ap()
    table = nc.dram_tensor("slot_token", ((BLOCKS + 1) * SLOTS, 1), I32).ap()
    io["slot_token"], io["slot_token_u"] = table, table.bitcast(U32)
    program(nc, io)
    result = run_bass_kernel_spmd(nc, [arrays], core_ids=[0])
    return result.results[0]["out_y"]
```

```python
from contextlib import ExitStack

import concourse.bass as bass
from concourse import mybir

F32 = mybir.dt.float32
I32 = mybir.dt.int32
U32 = mybir.dt.uint32
ALU = mybir.AluOpType
ACT = mybir.ActivationFunctionType
AX = mybir.AxisListType

P = 128
D = 1024
SEQ = 1024
META = 16
KEYS = SEQ + META
TILES = SEQ // P
MT = TILES
DC = D // P
EPS = 1e-6

SWA_HEADS, SWA_KV, HD = 8, 2, 64
PAIRS = SWA_HEADS // SWA_KV
BAND = 3 * P + META
MLA_HEADS, NOPE, ROPE, VD = 8, 64, 32, 64
QK = NOPE + ROPE
Q_LORA, KV_LORA = 256, 128
C_K, C_V, C_QL = 512, 640, 768
C_KVL, C_KR, C_END = 1024, 1152, 1184
PROJ = [(0, 512), (1024, C_END), (512, 1024)]

E, TOPK, FF = 32, 4, 1024
FC = FF // P
SLOTS = 176
WIDTHS = (124, 128, 132, 136, 144, 152, 160, SLOTS)
HALF = SLOTS // 2
GROUP = 8
ROUNDS = -(-SEQ // SLOTS)
MOST = (SEQ * TOPK - E) // SLOTS + E
BLOCKS = -(-MOST // GROUP) * GROUP
LEAST = -(-SEQ * TOPK // SLOTS)
LIMIT, ALPHA = 7.0, 1.702


def rows(t):
    return P if t < MT else META


def cols(t):
    return slice(t * P, t * P + rows(t))


def spread(ap, n):
    return ap.unsqueeze(2).to_broadcast([ap.shape[0], ap.shape[1], n])


def repeat(ap, n):
    return ap.unsqueeze(1).to_broadcast([ap.shape[0], n, ap.shape[1]])


class Mem:

    def __init__(self, nc, ctx):
        self.nc, self.ctx = nc, ctx

    def sb(self, name, shape, dt=F32):
        return self.ctx.enter_context(self.nc.sbuf_tensor(name, shape, dt))

    def ps(self, name, shape):
        return self.ctx.enter_context(self.nc.psum_tensor(name, shape, F32))

    def sem(self, name):
        return self.ctx.enter_context(self.nc.semaphore(name))


def chain(eng, sem):
    count = [0]

    def link(ins):
        count[0] += 1
        ins.then_inc(sem, 1)
        eng.wait_ge(sem, count[0])

    return link


def project(nc, io, keep):
    with ExitStack() as ctx:
        m = Mem(nc, ctx)
        w_in = m.sb("w_in_sb", [P, DC, C_END])
        w_qup = m.sb("w_qup", [P, Q_LORA // P, MLA_HEADS * QK])
        w_kvup = m.sb("w_kvup", [P, MLA_HEADS * (NOPE + VD)])
        g_attn = m.sb("g_attn", [P, DC])
        g_ql = m.sb("g_ql", [P, Q_LORA // P])
        g_kvl = m.sb("g_kvl", [P, 1])
        swa_g = m.sb("swa_g", [P, 2])
        mla_g = m.sb("mla_g", [QK, 2])
        g_rot = m.sb("g_rot", [P, 2, ROPE])
        cos_q = m.sb("cos_q", [P, MT, ROPE])
        sin_q = m.sb("sin_q", [P, MT, ROPE])
        cos_k = m.sb("cos_k", [P, MT + 1, ROPE])
        sin_k = m.sb("sin_k", [P, MT + 1, ROPE])
        inv_n = m.sb("inv_n", [P, 12])
        xt = m.sb("xt", [P, 3, D])
        square = m.sb("square", [P, D], mybir.dt.bfloat16)
        normT = m.sb("normT", [P, 2, DC, P])
        proj = m.sb("proj", [P, 2, C_END])
        proj_sq = m.sb("proj_sq", [P, C_END])
        up_sq = proj_sq[:, 0:MLA_HEADS * QK].rearrange("p (h c) -> p h c", c=QK)
        x_stat = m.sb("x_stat", [P, MT + 1, 3])
        stat = m.sb("stat", [P, 12])
        stat_root = m.sb("stat_root", [P, 12])
        stat_inv = stat_root
        kr_sq = m.sb("kr_sq", [P, 1])
        qn = m.sb("qn", [P, PAIRS, SWA_KV, HD])
        lat = m.sb("lat", [P, 4, P])
        latT = m.sb("latT", [P, 3, P])
        k_raw = m.sb("k_raw", [P, MLA_HEADS, QK])
        q_raw = m.sb("q_raw", [P, MLA_HEADS, QK])
        head_stat = m.sb("head_stat", [P, 2 * MLA_HEADS])
        head_root = m.sb("head_root", [P, 2 * MLA_HEADS])
        head_inv = head_root
        k_rot = m.sb("k_rot", [P, ROPE])
        k_rot2 = proj_sq[:, 0:ROPE]
        wide = MLA_HEADS * ROPE
        q_rot = proj_sq[:, MLA_HEADS * QK:MLA_HEADS * QK + wide].rearrange("p (h c) -> p h c", c=ROPE)
        q_rot2 = proj_sq[:, 0:wide].rearrange("p (h c) -> p h c", c=ROPE)
        xT_bank = m.ps("xT_bank", [P, 2, 512])
        proj_bank = m.ps("proj_bank", [P, 3, 512])
        job_bank = m.ps("job_bank", [P, 3, 512])
        swa_qT, swa_kT, swa_v = keep["swa_qT"], keep["swa_kT"], keep["swa_v"]
        mla_qT, mla_kT, mla_v = keep["mla_qT"], keep["mla_kT"], keep["mla_v"]
        ident = keep["ident"]

        ident_in = m.sem("ident_in")
        g_attn_in = m.sem("g_attn_in")
        const_in = m.sem("const_in")
        w_in_in = [m.sem(f"w_in_in{k}") for k in range(DC)]
        gains_set = m.sem("gains_set")
        gains_one = m.sem("gains_one")
        x_in = [m.sem(f"x_in{i}") for i in range(3)]
        x_root = m.sem("x_root")
        x_normed = m.sem("x_normed")
        w_scaled = m.sem("w_scaled")
        xT_done = m.sem("xT_done")
        normT_lo = m.sem("normT_lo")
        normT_hi = m.sem("normT_hi")
        proj_done = m.sem("proj_done")
        proj_out = m.sem("proj_out")
        v_copied = m.sem("v_copied")
        stat_ready = m.sem("stat_ready")
        root_ready = m.sem("root_ready")
        lat_ready = m.sem("lat_ready")
        head_stat_ready = m.sem("head_stat_ready")
        head_root_ready = m.sem("head_root_ready")
        k_ready = m.sem("k_ready")
        q_ready = m.sem("q_ready")
        job_done = m.sem("job_done")
        job_out = m.sem("job_out")
        act_own = m.sem("act_own_p")
        dve_own = m.sem("dve_own_p")
        pool_own = m.sem("pool_own_p")

        jobs = []
        for t in range(MT + 1):
            names = ("qpairs", "lats", "kv0", "kv1", "q0", "q1", "kT0", "kT1", "qT0", "qT1")
            jobs += [(t, n) for n in names if t < MT or n in ("lats", "kv0", "kv1", "kT0", "kT1")]
        place = {job: j for j, job in enumerate(jobs)}

        consts = [
            (g_ql[:], io["mla_q_lat_norm_g"][0].rearrange("(k p) -> p k", p=P)),
            (g_kvl[:], io["mla_kv_lat_norm_g"][0].rearrange("(k p) -> p k", p=P)),
            (swa_g[0:HD, 0:1], io["swa_q_norm_g"][0].rearrange("(k p) -> p k", p=HD)),
            (swa_g[HD:P, 0:1], io["swa_q_norm_g"][0].rearrange("(k p) -> p k", p=HD)),
            (swa_g[0:HD, 1:2], io["swa_k_norm_g"][0].rearrange("(k p) -> p k", p=HD)),
            (swa_g[HD:P, 1:2], io["swa_k_norm_g"][0].rearrange("(k p) -> p k", p=HD)),
            (g_rot[:, 0, :], io["mla_q_norm_g"][0, NOPE:QK].partition_broadcast(P)),
            (g_rot[:, 1, :], io["mla_k_norm_g"][0, NOPE:QK].partition_broadcast(P)),
            (cos_k[:], io["cos2"]),
            (sin_k[:], io["sin2"]),
            (inv_n[:], io["inv_n"]),
            (w_qup[:], io["w_mla_q_up"][0].rearrange("(k p) n -> p k n", p=P)),
            (w_kvup[:], io["w_mla_kv_up"][0]),
        ]
        gain_cols = [
            (mla_g[0:NOPE, 0:1], io["mla_q_norm_g"][0, 0:NOPE].rearrange("(k p) -> p k", p=NOPE)),
            (mla_g[0:NOPE, 1:2], io["mla_k_norm_g"][0, 0:NOPE].rearrange("(k p) -> p k", p=NOPE)),
        ]
        CONSTS = 16 * (len(consts) + len(gain_cols))

        with nc.Block() as block:

            @block.sync
            def _(sp):
                def load_x(t):
                    if t >= 3:
                        sp.wait_ge(xT_done, 2 * (t - 2))
                    src = io["meta_tokens"] if t == MT else io["x"][0, t * P:(t + 1) * P, :]
                    sp.dma_start(xt[0:rows(t), t % 3, :], src).then_inc(x_in[t % 3], 16)

                load_x(0)
                for k in range(DC):
                    sp.dma_start(w_in[:, k, :], io["w_in"][0, k * P:(k + 1) * P, :]).then_inc(w_in_in[k], 16)
                for t in range(1, MT + 1):
                    load_x(t)

            @block.gpsimd
            def _(pool):
                nc.gpsimd.memset(mla_g[:], 1.0).then_inc(gains_one, 1)
                for t in range(MT + 1):
                    n = rows(t)
                    pool.wait_ge(proj_out, 3 * t + 3)
                    nc.gpsimd.tensor_copy(swa_v[0:n, t, :], proj[0:n, t % 2, C_V:C_QL]).then_inc(v_copied, 1)

            @block.scalar
            def _(act):
                link = chain(act, act_own)
                with nc.allow_non_contiguous_dma(reason="gains to one per partition, a few KiB in all"):
                    act.dma_start(ident[:], io["ident"]).then_inc(ident_in, 16)
                    act.dma_start(g_attn[:], io["attn_norm_g"][0].rearrange("(k p) -> p k", p=P))\
                        .then_inc(g_attn_in, 16)

                def x_stats(t):
                    n = rows(t)
                    act.wait_ge(x_in[t % 3], 16 * (t // 3 + 1))
                    link(nc.scalar.activation(square[0:n, :], xt[0:n, t % 3, :], ACT.Square,
                                              accum_out=x_stat[0:n, t, 0:1]))
                    nc.scalar.activation(x_stat[0:n, t, 1:2], x_stat[0:n, t, 0:1], ACT.Sqrt,
                                         scale=1.0 / D, bias=keep["eps"][0:n, :]).then_inc(x_root, 1)

                def proj_copy(t, part):
                    n = rows(t)
                    c0, c1 = PROJ[part]
                    if part == 0 and t >= 2:
                        act.wait_ge(lat_ready, t - 1)
                        act.wait_ge(v_copied, t - 1)
                    act.wait_ge(proj_done, 3 * t + part + 1)
                    nc.scalar.copy(proj[0:n, t % 2, c0:c1], proj_bank[0:n, part, 0:c1 - c0]).then_inc(proj_out, 1)

                def job(t, name):
                    j, n = place[t, name], rows(t)
                    bank = job_bank[:, j % 3, :]
                    act.wait_ge(job_done, j + 1)
                    h = 4 * int(name[-1]) if name[-1] in "01" else 0
                    if name == "qpairs":
                        last = nc.scalar.activation(
                            swa_qT[:, :, cols(t)], bank.rearrange("p (j q) -> p j q", q=P),
                            ACT.Copy, scale=swa_g[:, 0:1])
                    elif name == "lats":
                        nc.scalar.copy(swa_kT[:, cols(t)], bank[:, 0:n])
                        a = 0 if t < MT else 2
                        last = nc.scalar.copy(latT[:, a:3, 0:n],
                                              bank.rearrange("p (j q) -> p j q", q=P)[:, 1 + a:4, 0:n])
                    elif name in ("kv0", "kv1"):
                        kv = bank.rearrange("p (h c) -> p h c", c=NOPE + VD)
                        nc.scalar.copy(k_raw[0:n, h:h + 4, 0:NOPE], kv[0:n, :, 0:NOPE])
                        last = nc.scalar.copy(mla_v[0:n, t, h:h + 4, :], kv[0:n, :, NOPE:NOPE + VD])
                    elif name in ("q0", "q1"):
                        last = nc.scalar.copy(q_raw[:, h:h + 4, :],
                                              bank[:, 0:4 * QK].rearrange("p (h c) -> p h c", c=QK))
                    elif name in ("kT0", "kT1"):
                        last = nc.scalar.copy(mla_kT[:, h:h + 4, cols(t)],
                                              bank.rearrange("p (h q) -> p h q", q=P)[0:QK, :, 0:n])
                    else:
                        last = nc.scalar.activation(
                            mla_qT[:, h:h + 4, cols(t)], bank.rearrange("p (h q) -> p h q", q=P)[0:QK, :, :],
                            ACT.Copy, scale=mla_g[:, 0:1])
                    last.then_inc(job_out, 1)

                def norm_copy(t):
                    if t >= 2:
                        act.wait_ge(proj_done, 3 * (t - 1))
                    act.wait_ge(xT_done, 2 * t + 1)
                    nc.scalar.copy(normT[:, t % 2, 0:4, 0:rows(t)],
                                   xT_bank[:, 0, :].rearrange("p (k q) -> p k q", q=P)[:, :, 0:rows(t)])\
                        .then_inc(normT_lo, 1)

                x_stats(0)
                with nc.allow_non_contiguous_dma(reason="gains to one per partition, a few KiB in all"):
                    for dst, src in consts:
                        act.dma_start(dst, src).then_inc(const_in, 16)
                    act.wait_ge(gains_one, 1)
                    for dst, src in gain_cols:
                        act.dma_start(dst, src).then_inc(const_in, 16)
                norm_copy(0)
                x_stats(1)
                for s in range(-1, MT + 1):
                    if s >= 0:
                        n = rows(s)
                        if s + 2 <= MT:
                            x_stats(s + 2)
                        act.wait_ge(stat_ready, s + 1)
                        nc.scalar.activation(stat_root[0:n, :], stat[0:n, :], ACT.Sqrt,
                                             bias=keep["eps"][0:n, :]).then_inc(root_ready, 1)
                    if s + 1 <= MT:
                        proj_copy(s + 1, 0)
                    if s >= 0:
                        if s < MT:
                            if s == 0:
                                act.wait_ge(gains_set, 1)
                            job(s, "qpairs")
                        job(s, "lats")
                    if s + 1 <= MT:
                        proj_copy(s + 1, 1)
                    if s >= 0:
                        for name in ("kv0", "kv1") + (("q0", "q1") if s < MT else ()):
                            job(s, name)
                        act.wait_ge(head_stat_ready, s + 1)
                        nc.scalar.activation(head_root[0:n, :], head_stat[0:n, :], ACT.Sqrt,
                                             bias=keep["eps"][0:n, :]).then_inc(head_root_ready, 1)
                    if s + 1 <= MT:
                        proj_copy(s + 1, 2)
                    if s + 2 <= MT:
                        norm_copy(s + 2)
                    if s >= 0:
                        for name in ("kT0", "kT1") + (("qT0", "qT1") if s < MT else ()):
                            job(s, name)

            @block.vector
            def _(dve):
                link = chain(dve, dve_own)
                v = nc.vector

                def x_norm(t):
                    n = rows(t)
                    dve.wait_ge(x_root, t + 1)
                    link(v.reciprocal(x_stat[0:n, t, 2:3], x_stat[0:n, t, 1:2]))
                    v.tensor_scalar(xt[0:n, t % 3, :], xt[0:n, t % 3, :], x_stat[0:n, t, 2:3], None,
                                    ALU.mult).then_inc(x_normed, 1)

                def norm_copy(t):
                    if t >= 2:
                        dve.wait_ge(proj_done, 3 * (t - 1))
                    dve.wait_ge(xT_done, 2 * t + 2)
                    v.tensor_copy(normT[:, t % 2, 4:8, 0:rows(t)],
                                  xT_bank[:, 1, :].rearrange("p (k q) -> p k q", q=P)[:, :, 0:rows(t)])\
                        .then_inc(normT_hi, 1)

                x_norm(0)
                dve.wait_ge(g_attn_in, 16)
                for k in range(DC):
                    dve.wait_ge(w_in_in[k], 16)
                    v.tensor_scalar(w_in[:, k, :], w_in[:, k, :], g_attn[:, k:k + 1], None, ALU.mult)\
                        .then_inc(w_scaled, 1)
                    if k == 1:
                        norm_copy(0)
                dve.wait_ge(const_in, CONSTS)
                link(v.tensor_tensor(swa_g[:, 0:1], swa_g[:, 0:1], swa_g[:, 1:2], ALU.mult))
                v.tensor_scalar(swa_g[:, 0:1], swa_g[:, 0:1], float(HD) ** -0.5, None, ALU.mult)
                link(v.tensor_tensor(mla_g[:, 0:1], mla_g[:, 0:1], mla_g[:, 1:2], ALU.mult))
                v.tensor_scalar(mla_g[:, 0:1], mla_g[:, 0:1], float(QK) ** -0.5, None, ALU.mult)
                half = ROPE // 2
                for i, (c, s, n) in enumerate(((cos_q, sin_q, MT), (cos_k, sin_k, MT + 1))):
                    v.tensor_tensor(c[:], cos_k[:, 0:n, :], repeat(g_rot[:, i, :], n), ALU.mult)
                    v.tensor_tensor(s[:, :, 0:half], sin_k[:, 0:n, 0:half], repeat(g_rot[:, i, half:ROPE], n), ALU.mult)
                    link(v.tensor_tensor(s[:, :, half:ROPE], sin_k[:, 0:n, half:ROPE],
                                         repeat(g_rot[:, i, 0:half], n), ALU.mult))
                v.memset(head_stat[:], 1.0)
                for k in range(Q_LORA // P):
                    v.tensor_scalar(w_qup[:, k, :], w_qup[:, k, :], g_ql[:, k:k + 1], None, ALU.mult)
                v.tensor_scalar(w_kvup[:], w_kvup[:], g_kvl[:, 0:1], None, ALU.mult).then_inc(gains_set, 1)

                def rotate(out, tmp, src, cos, sin):
                    v.tensor_tensor(out, src, cos, ALU.mult)
                    lo, hi = (slice(None),) * (len(src.shape) - 1) + (slice(0, half),), \
                        (slice(None),) * (len(src.shape) - 1) + (slice(half, ROPE),)
                    v.tensor_tensor(tmp[lo], src[hi], sin[lo], ALU.mult)
                    link(v.tensor_tensor(tmp[hi], src[lo], sin[hi], ALU.mult))
                    link(v.tensor_tensor(out, out, tmp, ALU.add))

                x_norm(1)
                norm_copy(1)
                for s in range(MT + 1):
                    if s + 2 <= MT:
                        x_norm(s + 2)
                    n = rows(s)
                    pr = proj[0:n, s % 2, :]
                    dve.wait_ge(proj_out, 3 * (s + 1))
                    if s >= 1:
                        dve.wait_ge(q_ready, s)
                    link(v.tensor_tensor(proj_sq[0:n, :], pr, pr, ALU.mult))
                    v.tensor_reduce(stat[0:n, 0:10], proj_sq[0:n, 0:C_V].rearrange("p (h c) -> p h c", c=HD),
                                    AX.X, ALU.add)
                    v.tensor_reduce(stat[0:n, 10:11], proj_sq[0:n, C_QL:C_KVL], AX.X, ALU.add)
                    v.tensor_reduce(stat[0:n, 11:12], proj_sq[0:n, C_KVL:C_KR], AX.X, ALU.add)
                    link(v.tensor_reduce(kr_sq[0:n, :], proj_sq[0:n, C_KR:C_END], AX.X, ALU.add))
                    v.tensor_tensor(stat[0:n, :], stat[0:n, :], inv_n[0:n, :], ALU.mult).then_inc(stat_ready, 1)
                    rotate(k_rot[0:n, :], k_rot2[0:n], pr[:, C_KR:C_END], cos_k[0:n, s, :], sin_k[0:n, s, :])
                    dve.wait_ge(root_ready, s + 1)
                    link(v.reciprocal(stat_inv[0:n, :], stat_root[0:n, :]))
                    if s < MT:
                        for g in range(SWA_KV):
                            v.tensor_tensor(
                                qn[:, :, g, :],
                                pr[:, g * PAIRS * HD:(g + 1) * PAIRS * HD].rearrange("p (j c) -> p j c", c=HD),
                                spread(stat_inv[:, g * PAIRS:(g + 1) * PAIRS], HD), ALU.mult)
                        v.tensor_scalar(lat[:, 1:3, :], pr[:, C_QL:C_KVL].rearrange("p (k c) -> p k c", c=P),
                                        stat_inv[:, 10:11], None, ALU.mult)
                    v.tensor_tensor(lat[0:n, 0, :].rearrange("p (g c) -> p g c", c=HD),
                                    pr[:, C_K:C_V].rearrange("p (g c) -> p g c", c=HD),
                                    spread(stat_inv[0:n, 8:10], HD), ALU.mult)
                    v.tensor_scalar(lat[0:n, 3, :], pr[:, C_KVL:C_KR], stat_inv[0:n, 11:12], None, ALU.mult)\
                        .then_inc(lat_ready, 1)

                    H = MLA_HEADS
                    dve.wait_ge(job_out, place[s, "kv1"] + 1)
                    own = k_raw[0:n, :, 0:NOPE]
                    link(v.tensor_tensor(up_sq[0:n, :, 0:NOPE], own, own, ALU.mult))
                    link(v.tensor_reduce(head_stat[0:n, 0:H], up_sq[0:n, :, 0:NOPE], AX.X, ALU.add))
                    last = v.tensor_scalar(head_stat[0:n, 0:H], head_stat[0:n, 0:H], kr_sq[0:n, 0:1], 1.0 / QK,
                                           ALU.add, ALU.mult)
                    if s < MT:
                        dve.wait_ge(job_out, place[s, "q1"] + 1)
                        link(v.tensor_tensor(up_sq, q_raw[:], q_raw[:], ALU.mult))
                        link(v.tensor_reduce(head_stat[:, H:2 * H], up_sq, AX.X, ALU.add))
                        last = v.tensor_scalar(head_stat[:, H:2 * H], head_stat[:, H:2 * H], 1.0 / QK, None, ALU.mult)
                    last.then_inc(head_stat_ready, 1)
                    if s < MT:
                        rotate(q_rot, q_rot2, q_raw[:, :, NOPE:QK], repeat(cos_q[:, s, :], H),
                               repeat(sin_q[:, s, :], H))
                    dve.wait_ge(head_root_ready, s + 1)
                    link(v.reciprocal(head_inv[0:n, :], head_root[0:n, :]))
                    v.tensor_tensor(own, own, spread(head_inv[0:n, 0:H], NOPE), ALU.mult)
                    v.tensor_tensor(k_raw[0:n, :, NOPE:QK], repeat(k_rot[0:n, :], H),
                                    spread(head_inv[0:n, 0:H], ROPE), ALU.mult).then_inc(k_ready, 1)
                    if s < MT:
                        v.tensor_tensor(q_raw[:, :, 0:NOPE], q_raw[:, :, 0:NOPE],
                                        spread(head_inv[:, H:2 * H], NOPE), ALU.mult)
                        v.tensor_tensor(q_raw[:, :, NOPE:QK], q_rot, spread(head_inv[:, H:2 * H], ROPE),
                                        ALU.mult).then_inc(q_ready, 1)
                    if s + 2 <= MT:
                        norm_copy(s + 2)

            @block.tensor
            def _(pe):
                def start_job(t, name):
                    j = place[t, name]
                    if j >= 3:
                        pe.wait_ge(job_out, j - 2)
                    return job_bank[:, j % 3, :]

                def transposes(t, name, parts):
                    bank = start_job(t, name)
                    n = rows(t)
                    for i, part in parts:
                        w = part.shape[-1]
                        last = nc.tensor.transpose(bank[0:w, i * P:i * P + n], part, ident[0:n, 0:n])
                    last.then_inc(job_done, 1)

                def proj_part(t, part):
                    n = rows(t)
                    c0, c1 = PROJ[part]
                    if t >= 1:
                        pe.wait_ge(proj_out, 3 * (t - 1) + part + 1)
                    for k in range(DC):
                        last = nc.tensor.matmul(proj_bank[0:n, part, 0:c1 - c0], normT[:, t % 2, k, 0:n],
                                                w_in[:, k, c0:c1], start=(k == 0), stop=(k == DC - 1))
                    last.then_inc(proj_done, 1)

                def transpose_x(t):
                    n = rows(t)
                    pe.wait_ge(x_normed, t + 1)
                    for b, freed in ((0, normT_lo), (1, normT_hi)):
                        if t >= 1:
                            pe.wait_ge(freed, t)
                        for k in range(4):
                            c = (4 * b + k) * P
                            last = nc.tensor.transpose(xT_bank[:, b, k * P:k * P + n],
                                                       xt[0:n, t % 3, c:c + P], ident[0:n, 0:n])
                        last.then_inc(xT_done, 1)

                pe.wait_ge(ident_in, 16)
                transpose_x(0)
                for s in range(-1, MT + 1):
                    n = rows(max(s, 0))
                    if s + 1 <= MT:
                        pe.wait_ge(normT_lo, s + 2)
                        pe.wait_ge(normT_hi, s + 2)
                        if s == -1:
                            pe.wait_ge(w_scaled, DC)
                        proj_part(s + 1, 0)
                    if s >= 0:
                        pe.wait_ge(lat_ready, s + 1)
                        if s < MT:
                            transposes(s, "qpairs", [(j, qn[:, j, :, :].rearrange("p g c -> p (g c)"))
                                                     for j in range(PAIRS)])
                        transposes(s, "lats", [(i, lat[0:n, i, :]) for i in ((0, 1, 2, 3) if s < MT else (0, 3))])
                    if s + 1 <= MT:
                        proj_part(s + 1, 1)
                    if s >= 0:
                        pe.wait_ge(job_out, place[s, "lats"] + 1)
                        if s == 0:
                            pe.wait_ge(gains_set, 1)
                        for hf in range(2):
                            bank = start_job(s, f"kv{hf}")
                            nc.tensor.matmul(bank[0:n, :], latT[:, 2, 0:n], w_kvup[:, hf * 512:(hf + 1) * 512],
                                             start=True, stop=True).then_inc(job_done, 1)
                        for hf in range(2) if s < MT else ():
                            bank = start_job(s, f"q{hf}")
                            for k in range(2):
                                last = nc.tensor.matmul(bank[:, 0:4 * QK], latT[:, k, :],
                                                        w_qup[:, k, hf * 4 * QK:(hf + 1) * 4 * QK],
                                                        start=(k == 0), stop=(k == 1))
                            last.then_inc(job_done, 1)
                    if s + 1 <= MT:
                        proj_part(s + 1, 2)
                    if s + 2 <= MT:
                        transpose_x(s + 2)
                    if s >= 0:
                        pe.wait_ge(k_ready, s + 1)
                        for hf in range(2):
                            transposes(s, f"kT{hf}", [(i, k_raw[0:n, 4 * hf + i, :]) for i in range(4)])
                        if s < MT:
                            pe.wait_ge(q_ready, s + 1)
                            for hf in range(2):
                                transposes(s, f"qT{hf}", [(i, q_raw[:, 4 * hf + i, :]) for i in range(4)])


def window(t):
    return (P if t == 0 else 0), (BAND - P if t == TILES - 1 else BAND)


def attend(nc, io, keep):
    UNITS = MLA_HEADS + SWA_HEADS
    with ExitStack() as ctx:
        m = Mem(nc, ctx)
        w_out = m.sb("w_out_sb", [P, DC, D])
        band_bias = m.sb("band_bias", [P, SWA_HEADS, BAND])
        sink = m.sb("sink", [P, SWA_HEADS])
        no_rows = m.sb("no_rows", [HALF, 2 * D])
        v_meta = m.sb("v_meta", [P, MLA_HEADS, VD])
        resid = m.sb("resid", [P, 2, D])
        probs = m.sb("probs", [P, 2, SEQ])
        probsT = m.sb("probsT", [P, 2, DC, P])
        biased = m.sb("biased", [P, 2, BAND])
        meta_s = m.sb("meta_s", [P, 2, MLA_HEADS, META])
        meta_p = m.sb("meta_p", [P, MLA_HEADS * META])
        meta_pT = m.sb("meta_pT", [P, P])
        meta_max = m.sb("meta_max", [P, 2, MLA_HEADS])
        real_max = m.sb("real_max", [P, 2])
        neg_max = m.sb("neg_max", [P, 2])
        band_max = m.sb("band_max", [P, SWA_HEADS])
        neg_band = m.sb("neg_band", [P, SWA_HEADS])
        real_sum = m.sb("real_sum", [P, MLA_HEADS])
        meta_sum = m.sb("meta_sum", [P, MLA_HEADS])
        band_sum = m.sb("band_sum", [P, SWA_HEADS])
        sink_exp = m.sb("sink_exp", [P, SWA_HEADS])
        mla_inv = m.sb("mla_inv", [P, MLA_HEADS])
        swa_inv = m.sb("swa_inv", [P, SWA_HEADS])
        mixed = m.sb("mixed", [P, 2 * 512])
        mixedT = m.sb("mixedT", [P, DC, P])
        score_bank = m.ps("score_bank", [P, 2, 1024])
        act_bank = m.ps("act_bank", [P, 512])
        dve_bank = m.ps("dve_bank", [P, 512])
        mla_bank = m.ps("mla_bank", [P, 512])
        swa_bank = m.ps("swa_bank", [P, 512])
        swa_qT, swa_kT, swa_v = keep["swa_qT"], keep["swa_kT"], keep["swa_v"]
        mla_qT, mla_kT, mla_v = keep["mla_qT"], keep["mla_kT"], keep["mla_v"]
        ident = keep["ident"]

        const_in = m.sem("const_in_a")
        w_out_in = m.sem("w_out_in")
        v_meta_zero = m.sem("v_meta_zero")
        no_rows_set = m.sem("no_rows_set")
        y_zeroed = m.sem("y_zeroed")
        v_meta_in = m.sem("v_meta_in")
        resid_in = [m.sem(f"resid_in{i}") for i in range(2)]
        resid_out = [m.sem(f"resid_out{i}") for i in range(2)]
        scores_done = m.sem("scores_done")
        max_ready = m.sem("max_ready")
        band_ready = m.sem("band_ready")
        exp_done = m.sem("exp_done")
        meta_done = m.sem("meta_done")
        meta_read = m.sem("meta_read")
        act_T_done = m.sem("act_T_done")
        act_T_out = m.sem("act_T_out")
        dve_T_done = m.sem("dve_T_done")
        dve_T_out = m.sem("dve_T_out")
        values_done = m.sem("values_done")
        mla_done = m.sem("mla_done")
        mla_mixed = m.sem("mla_mixed")
        swa_mixed = m.sem("swa_mixed")
        sink_diff = m.sem("sink_diff")
        sink_done = m.sem("sink_done")
        attn_added = m.sem("attn_added")
        dve_own = m.sem("dve_own_a")

        fills, act_T, dve_T = [], [], []
        for n in range(TILES * UNITS + 8):
            t, i = divmod(n, UNITS)
            if t < TILES:
                fills.append(("unit", n))
            if 0 < n <= TILES * UNITS:
                mla = (n - 1) % UNITS < MLA_HEADS
                if mla:
                    act_T.append(("unit", n - 1))
                dve_T.append(("unit", n - 1))
            if i == 9 and t < TILES:
                act_T.append(("meta", t))
            if i == 3 and t >= 1:
                act_T.append(("mixed", t - 1))
                dve_T.append(("mixed", t - 1))
            if i == 5 and t >= 1:
                fills.append(("out", t - 1))
        at_fill = {x: j for j, x in enumerate(fills)}
        at_act = {x: j for j, x in enumerate(act_T)}
        at_dve = {x: j for j, x in enumerate(dve_T)}

        def band_units(n):
            t, i = divmod(n, UNITS)
            return t * SWA_HEADS + max(0, i + 1 - MLA_HEADS)

        def wait_fill_free(eng, j):
            if j < 2:
                return
            kind, n = fills[j - 2]
            if kind == "out":
                eng.wait_ge(attn_added, n + 1)
            elif n % UNITS < MLA_HEADS:
                eng.wait_ge(exp_done, n + 1)
            else:
                eng.wait_ge(band_ready, band_units(n))

        def band_parts(t):
            first, _ = window(t)
            parts = []
            if t > 0:
                parts.append((0 - first, (t - 1) * P, P, t - 1))
            parts.append((P - first, SEQ, META, MT))
            parts.append((P + META - first, t * P, P, t))
            if t < TILES - 1:
                parts.append((2 * P + META - first, (t + 1) * P, P, t + 1))
            whole = [x for x in parts if x[2] == P] + [x for x in parts if x[2] != P]
            return [(*x, j) for j, x in enumerate(whole)]

        with nc.Block() as block:

            @block.sync
            def _(sp):
                sp.dma_start(band_bias[:], io["band_bias"]).then_inc(const_in, 16)
                sp.dma_start(sink[:], io["swa_sink"][0].partition_broadcast(P)).then_inc(const_in, 16)
                sp.wait_ge(v_meta_zero, 1)
                for h in range(MLA_HEADS):
                    sp.dma_start(v_meta[h * META:(h + 1) * META, h, :], mla_v[0:META, MT, h, :]).then_inc(v_meta_in, 16)

                def load(t):
                    sp.dma_start(resid[:, t % 2, :], io["x"][0, t * P:(t + 1) * P, :]).then_inc(resid_in[t % 2], 16)

                load(0)
                load(1)
                sp.dma_start(w_out[:], io["w_out"][0].rearrange("(k p) n -> p k n", p=P)).then_inc(w_out_in, 16)
                for t in range(TILES):
                    sp.wait_ge(attn_added, t + 1)
                    sp.dma_start(io["h"][t * P:(t + 1) * P, :], resid[:, t % 2, :]).then_inc(resid_out[t % 2], 16)
                    if t + 2 < TILES:
                        sp.wait_ge(resid_out[t % 2], 16 * (t // 2 + 1))
                        load(t + 2)
                for b in range(2):
                    sp.wait_ge(resid_out[b], 16 * (TILES // 2))

            @block.gpsimd
            def _(pool):
                nc.gpsimd.memset(v_meta[:], 0.0).then_inc(v_meta_zero, 1)
                nc.gpsimd.memset(no_rows[:], 0.0).then_inc(no_rows_set, 1)
                pool.wait_ge(no_rows_set, 1)
                for b in range(LEAST + 1, BLOCKS + 1):
                    pool.dma_start(io["y"][b * SLOTS:(b + 1) * SLOTS, :].rearrange("(p j) d -> p (j d)", p=HALF),
                                   no_rows[:]).then_inc(y_zeroed, 16)
                pool.wait_ge(y_zeroed, 16 * (BLOCKS - LEAST))

            @block.scalar
            def _(act):
                def copy_T(key, out, src):
                    act.wait_ge(act_T_done, at_act[key] + 1)
                    nc.scalar.copy(out, src).then_inc(act_T_out, 1)

                for n in range(TILES * UNITS + 8):
                    t, i = divmod(n, UNITS)
                    u = n - 1
                    if 0 <= u < TILES * UNITS and u % UNITS < MLA_HEADS:
                        if u >= 2:
                            act.wait_ge(values_done, u - 1)
                        copy_T(("unit", u), probsT[:, u % 2, 0:4, :].rearrange("p k q -> p (k q)"), act_bank[:])
                    if i == 10 and t < TILES:
                        if t >= 1:
                            act.wait_ge(mla_done, t)
                        copy_T(("meta", t), meta_pT[:], act_bank[:, 0:P])
                    if i == 3 and t >= 1:
                        if t >= 2:
                            act.wait_ge(scores_done, at_fill["out", t - 2] + 1)
                        copy_T(("mixed", t - 1), mixedT[:, 0:4, :].rearrange("p k q -> p (k q)"), act_bank[:])
                    if i == 2 and t >= 1:
                        act.wait_ge(sink_diff, t)
                        nc.scalar.activation(sink_exp[:], sink_exp[:], ACT.Exp).then_inc(sink_done, 1)
                    if t >= TILES:
                        continue
                    j = at_fill["unit", n]
                    if n >= 2:
                        act.wait_ge(dve_T_done, at_dve["unit", n - 2] + 1)
                    if i < MLA_HEADS:
                        act.wait_ge(max_ready, t * MLA_HEADS + i + 1)
                        if i == 0 and t >= 1:
                            act.wait_ge(mla_mixed, t)
                        nc.scalar.activation(meta_p[:, i * META:(i + 1) * META], meta_s[:, t % 2, i, :], ACT.Exp,
                                             bias=neg_max[:, n % 2:n % 2 + 1], accum_out=meta_sum[:, i:i + 1])
                        nc.scalar.activation(probs[:, n % 2, :], score_bank[:, j % 2, :], ACT.Exp,
                                             bias=neg_max[:, n % 2:n % 2 + 1], accum_out=real_sum[:, i:i + 1])\
                            .then_inc(exp_done, 1)
                    else:
                        h = i - MLA_HEADS
                        w0, w1 = window(t)
                        act.wait_ge(band_ready, band_units(n))
                        if h == 0 and t >= 1:
                            act.wait_ge(swa_mixed, t)
                        nc.scalar.activation(probs[:, n % 2, 0:w1 - w0], biased[:, n % 2, 0:w1 - w0], ACT.Exp,
                                             bias=neg_band[:, h:h + 1], accum_out=band_sum[:, h:h + 1])\
                            .then_inc(exp_done, 1)

            @block.vector
            def _(dve):
                link = chain(dve, dve_own)
                v = nc.vector

                def take_meta(t):
                    if t >= 2:
                        dve.wait_ge(exp_done, (t - 2) * UNITS + MLA_HEADS)
                    dve.wait_ge(meta_done, t + 1)
                    v.tensor_copy(meta_s[:, t % 2, :, :].rearrange("p h c -> p (h c)"), swa_bank[:, 0:MLA_HEADS * META])
                    v.tensor_reduce(meta_max[:, t % 2, :],
                                    swa_bank[:, 0:MLA_HEADS * META].rearrange("p (h c) -> p h c", c=META),
                                    AX.X, ALU.max).then_inc(meta_read, 1)

                dve.wait_ge(const_in, 32)
                take_meta(0)
                for n in range(TILES * UNITS + 8):
                    t, i = divmod(n, UNITS)
                    if i == 6 and t >= 1:
                        j = at_fill["out", t - 1]
                        dve.wait_ge(resid_in[(t - 1) % 2], 16 * ((t - 1) // 2 + 1))
                        dve.wait_ge(scores_done, j + 1)
                        v.tensor_tensor(resid[:, (t - 1) % 2, :], resid[:, (t - 1) % 2, :], score_bank[:, j % 2, :],
                                        ALU.add).then_inc(attn_added, 1)
                    if t < TILES:
                        j = at_fill["unit", n]
                        dve.wait_ge(scores_done, j + 1)
                        if i < MLA_HEADS:
                            if i == 0:
                                dve.wait_ge(meta_read, t + 1)
                            link(v.tensor_reduce(real_max[:, n % 2:n % 2 + 1], score_bank[:, j % 2, :], AX.X, ALU.max))
                            if n >= 2:
                                dve.wait_ge(exp_done, n - 1)
                            v.tensor_scalar(neg_max[:, n % 2:n % 2 + 1], real_max[:, n % 2:n % 2 + 1],
                                            meta_max[:, t % 2, i:i + 1], -1.0, ALU.max, ALU.mult).then_inc(max_ready, 1)
                        else:
                            h = i - MLA_HEADS
                            w0, w1 = window(t)
                            dve.wait_ge(exp_done, n - 1)
                            link(v.tensor_tensor_reduce(out=biased[:, n % 2, 0:w1 - w0],
                                                        in0=score_bank[:, j % 2, 0:w1 - w0],
                                                        in1=band_bias[:, h, w0:w1], scale=1.0,
                                                        scalar=sink[:, h:h + 1], op0=ALU.add, op1=ALU.max,
                                                        accum_out=band_max[:, h:h + 1]))
                            v.tensor_scalar(neg_band[:, h:h + 1], band_max[:, h:h + 1], -1.0, None, ALU.mult)\
                                .then_inc(band_ready, 1)
                    u = n - 1
                    if 0 <= u < TILES * UNITS:
                        if u >= 2:
                            dve.wait_ge(values_done, u - 1)
                        dve.wait_ge(dve_T_done, at_dve["unit", u] + 1)
                        if u % UNITS < MLA_HEADS:
                            last = v.tensor_copy(probsT[:, u % 2, 4:8, :].rearrange("p k q -> p (k q)"), dve_bank[:])
                        else:
                            k = len(band_parts(u // UNITS)) - 1
                            v.tensor_copy(probsT[:, u % 2, 0:k, :].rearrange("p k q -> p (k q)"), dve_bank[:, 0:k * P])
                            last = v.tensor_copy(probsT[0:META, u % 2, k, :], dve_bank[0:META, k * P:(k + 1) * P])
                        last.then_inc(dve_T_out, 1)
                    if i == 6 and t + 1 < TILES:
                        take_meta(t + 1)
                    if i == 11 and t < TILES:
                        dve.wait_ge(mla_done, t + 1)
                        dve.wait_ge(exp_done, t * UNITS + MLA_HEADS)
                        link(v.tensor_tensor(mla_inv[:], real_sum[:], meta_sum[:], ALU.add))
                        link(v.reciprocal(mla_inv[:], mla_inv[:]))
                        v.tensor_tensor(mixed[:, 512:1024].rearrange("p (h c) -> p h c", c=VD),
                                        mla_bank[:].rearrange("p (h c) -> p h c", c=VD),
                                        spread(mla_inv[:], VD), ALU.mult).then_inc(mla_mixed, 1)
                    if i == 1 and t >= 1:
                        dve.wait_ge(exp_done, t * UNITS)
                        v.tensor_tensor(sink_exp[:], sink[:], neg_band[:], ALU.add).then_inc(sink_diff, 1)
                    if i == 2 and t >= 1:
                        dve.wait_ge(sink_done, t)
                        dve.wait_ge(values_done, t * UNITS)
                        link(v.tensor_tensor(swa_inv[:], band_sum[:], sink_exp[:], ALU.add))
                        link(v.reciprocal(swa_inv[:], swa_inv[:]))
                        v.tensor_tensor(mixed[:, 0:512].rearrange("p (h c) -> p h c", c=HD),
                                        swa_bank[:].rearrange("p (h c) -> p h c", c=HD),
                                        spread(swa_inv[:], HD), ALU.mult).then_inc(swa_mixed, 1)
                    if i == 3 and t >= 1:
                        dve.wait_ge(dve_T_done, at_dve["mixed", t - 1] + 1)
                        if t >= 2:
                            dve.wait_ge(scores_done, at_fill["out", t - 2] + 1)
                        v.tensor_copy(mixedT[:, 4:8, :].rearrange("p k q -> p (k q)"), dve_bank[:]).then_inc(dve_T_out, 1)

            @block.tensor
            def _(pe):
                def meta_scores(t):
                    if t >= 2:
                        pe.wait_ge(swa_mixed, t - 1)
                    for h in range(MLA_HEADS):
                        last = nc.tensor.matmul(swa_bank[:, h * META:(h + 1) * META], mla_qT[:, h, cols(t)],
                                                mla_kT[:, h, cols(MT)], start=True, stop=True)
                    last.then_inc(meta_done, 1)

                def scores(n):
                    t, i = divmod(n, UNITS)
                    j = at_fill["unit", n]
                    bank = score_bank[:, j % 2, :]
                    wait_fill_free(pe, j)
                    if i < MLA_HEADS:
                        for half in range(2):
                            last = nc.tensor.matmul(bank[:, half * 512:(half + 1) * 512], mla_qT[:, i, cols(t)],
                                                    mla_kT[:, i, half * 512:(half + 1) * 512], start=True, stop=True)
                    else:
                        g, pair = divmod(i - MLA_HEADS, PAIRS)
                        r = slice(g * HD, (g + 1) * HD)
                        for at, key, keys, _, _ in band_parts(t):
                            last = nc.tensor.matmul(bank[:, at:at + keys], swa_qT[r, pair, cols(t)],
                                                    swa_kT[r, key:key + keys], start=True, stop=True)
                    last.then_inc(scores_done, 1)

                def transpose_probs(n):
                    t, i = divmod(n, UNITS)
                    pe.wait_ge(exp_done, n + 1)
                    if i < MLA_HEADS:
                        if at_act["unit", n]:
                            pe.wait_ge(act_T_out, at_act["unit", n])
                        for k in range(4):
                            last = nc.tensor.transpose(act_bank[:, k * P:(k + 1) * P],
                                                       probs[:, n % 2, k * P:(k + 1) * P], ident[:])
                        last.then_inc(act_T_done, 1)
                    if at_dve["unit", n]:
                        pe.wait_ge(dve_T_out, at_dve["unit", n])
                    if i < MLA_HEADS:
                        for k in range(4):
                            last = nc.tensor.transpose(dve_bank[:, k * P:(k + 1) * P],
                                                       probs[:, n % 2, (4 + k) * P:(5 + k) * P], ident[:])
                    else:
                        for at, _, keys, _, slot in band_parts(t):
                            last = nc.tensor.transpose(dve_bank[0:keys, slot * P:(slot + 1) * P],
                                                       probs[:, n % 2, at:at + keys], ident[:])
                    last.then_inc(dve_T_done, 1)

                def values(n):
                    t, i = divmod(n, UNITS)
                    pe.wait_ge(dve_T_out, at_dve["unit", n] + 1)
                    if i < MLA_HEADS:
                        pe.wait_ge(act_T_out, at_act["unit", n] + 1)
                        if i == 0 and t >= 1:
                            pe.wait_ge(mla_mixed, t)
                        for k in range(DC):
                            last = nc.tensor.matmul(mla_bank[:, i * VD:(i + 1) * VD], probsT[:, n % 2, k, :],
                                                    mla_v[:, k, i, :], start=(i == 0 and k == 0), stop=False,
                                                    skip_group_check=True)
                    else:
                        h = i - MLA_HEADS
                        g = h // PAIRS
                        parts = band_parts(t)
                        if h == 0:
                            pe.wait_ge(meta_read, min(t + 2, TILES))
                        for x, (_, _, keys, kt, slot) in enumerate(parts):
                            last = nc.tensor.matmul(swa_bank[:, h * HD:(h + 1) * HD], probsT[0:keys, n % 2, slot, :],
                                                    swa_v[0:keys, kt, g * HD:(g + 1) * HD],
                                                    start=(x == 0), stop=(x == len(parts) - 1))
                    last.then_inc(values_done, 1)

                meta_scores(0)
                for n in range(TILES * UNITS + 8):
                    t, i = divmod(n, UNITS)
                    if i == 5 and t + 1 < TILES:
                        meta_scores(t + 1)
                    if t < TILES:
                        scores(n)
                    if 0 < n <= TILES * UNITS:
                        transpose_probs(n - 1)
                    if i == 9 and t < TILES:
                        pe.wait_ge(act_T_out, at_act["meta", t])
                        nc.tensor.transpose(act_bank[:, 0:P], meta_p[:], ident[:]).then_inc(act_T_done, 1)
                    if 1 < n <= TILES * UNITS + 1:
                        values(n - 2)
                    if i == 10 and t < TILES:
                        pe.wait_ge(act_T_out, at_act["meta", t] + 1)
                        if t == 0:
                            pe.wait_ge(v_meta_in, 16 * MLA_HEADS)
                        nc.tensor.matmul(mla_bank[:], meta_pT[:], v_meta[:].rearrange("p h c -> p (h c)"),
                                         start=False, stop=True, skip_group_check=True).then_inc(mla_done, 1)
                    if i == 3 and t >= 1:
                        pe.wait_ge(swa_mixed, t)
                        pe.wait_ge(mla_mixed, t)
                        for bank, out, done, key, c0 in ((act_bank, act_T_out, act_T_done, at_act["mixed", t - 1], 0),
                                                         (dve_bank, dve_T_out, dve_T_done, at_dve["mixed", t - 1], 4)):
                            pe.wait_ge(out, key)
                            for k in range(4):
                                c = (c0 + k) * P
                                last = nc.tensor.transpose(bank[:, k * P:(k + 1) * P], mixed[:, c:c + P], ident[:])
                            last.then_inc(done, 1)
                    if i == 5 and t >= 1:
                        j = at_fill["out", t - 1]
                        wait_fill_free(pe, j)
                        if t == 1:
                            pe.wait_ge(w_out_in, 16)
                        pe.wait_ge(act_T_out, at_act["mixed", t - 1] + 1)
                        pe.wait_ge(dve_T_out, at_dve["mixed", t - 1] + 1)
                        for half in range(2):
                            for k in range(DC):
                                last = nc.tensor.matmul(score_bank[:, j % 2, half * 512:(half + 1) * 512],
                                                        mixedT[:, k, :], w_out[:, k, half * 512:(half + 1) * 512],
                                                        start=(k == 0), stop=(k == DC - 1))
                        last.then_inc(scores_done, 1)


def route(nc, io, keep):
    with ExitStack() as ctx:
        m = Mem(nc, ctx)
        w_router = m.sb("w_router", [P, DC, E])
        b_router = m.sb("b_router", [P, E])
        g_ffn = m.sb("g_ffn", [P, D])
        tri = m.sb("tri", [P, P])
        ones = m.sb("ones", [P, P])
        expert_no = m.sb("expert_no", [P, E])
        block_no = m.sb("block_no", [P, BLOCKS + 1])
        token_no = m.sb("token_no", [P, TILES], I32)
        zeros = m.sb("zeros", [HALF, 2 * (BLOCKS + 2)], I32)
        ht = keep["h"]
        square = m.sb("square_r", [P, D])
        stat = m.sb("stat_r", [P, TILES, 3])
        normed = m.sb("normed_r", [P, 2, D])
        normT = m.sb("normT_r", [P, 2, DC, P])
        logits = m.sb("logits", [P, TILES, E])
        top = m.sb("top", [P, TILES, 8])
        top_i = m.sb("top_i", [P, TILES, 8], U32)
        top_f = m.sb("top_f", [P, TILES, TOPK])
        gate_sum = m.sb("gate_sum", [P, TILES])
        chosen = m.sb("chosen", [P, TOPK, TILES, E])
        sel = m.sb("sel", [P, TILES, E])
        before = m.sb("before", [P, TILES + 1, E])
        blocks = m.sb("blocks", [P, E])
        block_end = m.sb("block_end", [P, E])
        first_slot = m.sb("first_slot", [P, E])
        slot = m.sb("slot", [P, TILES, E])
        picked = m.sb("picked", [P, TOPK, TILES, E])
        slot_f = m.sb("slot_f", [P, TOPK, TILES])
        past = m.sb("past", [P, BLOCKS + 1, E])
        owner = m.sb("owner", [P, BLOCKS + 1])
        end_slot = m.sb("end_slot", [P, E])
        filled = m.sb("filled", [P, BLOCKS + 1])
        width_no = m.sb("width_no", [P, BLOCKS + 1])
        xT_bank = m.ps("xT_bank_r", [P, 2, 512])
        logit_bank = m.ps("logit_bank", [P, 2, 512])
        rank_bank = m.ps("rank_bank", [P, 512])
        count_bank = m.ps("count_bank", [P, 512])
        ident, gates, slot_i = keep["ident"], keep["gates"], keep["slot_i"]

        g_ffn_in = m.sem("g_ffn_in")
        const_in = m.sem("const_in_r")
        h_in = [m.sem(f"h_in{i}") for i in range(TILES)]
        h_root = m.sem("h_root")
        h_normed = m.sem("h_normed")
        rows_out = [m.sem(f"rows_out{i}") for i in range(2)]
        xT_done = m.sem("xT_done_r")
        normT_lo = m.sem("normT_lo_r")
        normT_hi = m.sem("normT_hi_r")
        logits_done = m.sem("logits_done")
        logits_read = m.sem("logits_read")
        gate_diff = m.sem("gate_diff")
        gate_exp = m.sem("gate_exp")
        sel_ready = m.sem("sel_ready")
        ranked = m.sem("ranked")
        zeroed = m.sem("zeroed")
        slots_ready = m.sem("slots_ready")
        scattered = m.sem("scattered")
        table_zero = m.sem("table_zero")
        dve_own = m.sem("dve_own_r")

        consts = [
            (w_router[:], io["router_w"][0].rearrange("(k p) n -> p k n", p=P)),
            (b_router[:], io["router_b"][0].partition_broadcast(P)),
            (tri[:], io["tri"]), (expert_no[:], io["expert_no"]),
            (block_no[:], io["block_no"]), (token_no[:], io["token_no"]),
        ]

        with nc.Block() as block:

            @block.sync
            def _(sp):
                for t in range(TILES):
                    sp.dma_start(ht[:, t, :], io["h"][t * P:(t + 1) * P, :]).then_inc(h_in[t], 16)
                for t in range(TILES):
                    sp.wait_ge(h_normed, t + 1)
                    sp.dma_start(io["rows"][t * P:(t + 1) * P, :], normed[:, t % 2, :]).then_inc(rows_out[t % 2], 16)
                for b in range(2):
                    sp.wait_ge(rows_out[b], 16 * (TILES // 2))

            @block.gpsimd
            def _(pool):
                nc.gpsimd.memset(zeros[:], 0).then_inc(zeroed, 1)
                pool.wait_ge(zeroed, 1)
                pool.dma_start(io["slot_token"].rearrange("(p c) one -> p (c one)", p=HALF), zeros[:])\
                    .then_inc(table_zero, 16)
                pool.wait_ge(table_zero, 16)
                pool.wait_ge(slots_ready, 1)
                for t in range(TILES):
                    for k in range(TOPK):
                        pool.indirect_dma_start(
                            out=io["slot_token"],
                            out_offset=bass.IndirectOffsetOnAxis(ap=slot_i[:, k, t:t + 1], axis=0),
                            in_=token_no[:, t:t + 1], in_offset=None,
                            bounds_check=(BLOCKS + 1) * SLOTS - 1, oob_is_err=False).then_inc(scattered, 16)
                pool.wait_ge(scattered, 16 * TILES * TOPK)

            @block.scalar
            def _(act):
                act.dma_start(g_ffn[:], io["ffn_norm_g"][0].partition_broadcast(P)).then_inc(g_ffn_in, 16)
                for dst, src in consts:
                    act.dma_start(dst, src).then_inc(const_in, 16)
                own = 0
                for t in range(TILES):
                    act.wait_ge(h_in[t], 16)
                    nc.scalar.activation(square[:], ht[:, t, :], ACT.Square, accum_out=stat[:, t, 0:1])\
                        .then_inc(keep["act_own"], 1)
                    own += 1
                    act.wait_ge(keep["act_own"], own)
                    nc.scalar.activation(stat[:, t, 1:2], stat[:, t, 0:1], ACT.Sqrt, scale=1.0 / D,
                                         bias=keep["eps"][:]).then_inc(h_root, 1)
                    if t >= 1:
                        act.wait_ge(xT_done, 2 * t - 1)
                        if t >= 3:
                            act.wait_ge(logits_done, t - 2)
                        nc.scalar.copy(normT[:, (t - 1) % 2, 0:4, :].rearrange("p k q -> p (k q)"), xT_bank[:, 0, :])\
                            .then_inc(normT_lo, 1)
                act.wait_ge(xT_done, 2 * TILES - 1)
                act.wait_ge(logits_done, TILES - 2)
                nc.scalar.copy(normT[:, (TILES - 1) % 2, 0:4, :].rearrange("p k q -> p (k q)"), xT_bank[:, 0, :])\
                    .then_inc(normT_lo, 1)
                act.wait_ge(gate_diff, 1)
                nc.scalar.activation(gates[:], gates[:], ACT.Exp).then_inc(gate_exp, 1)

            @block.vector
            def _(dve):
                link = chain(dve, dve_own)
                v = nc.vector

                def norm(t):
                    dve.wait_ge(h_root, t + 1)
                    link(v.reciprocal(stat[:, t, 2:3], stat[:, t, 1:2]))
                    if t >= 2:
                        dve.wait_ge(xT_done, 2 * (t - 1))
                        dve.wait_ge(rows_out[t % 2], 16 * (t // 2))
                    v.scalar_tensor_tensor(normed[:, t % 2, :], ht[:, t, :], stat[:, t, 2:3], g_ffn[:],
                                           ALU.mult, ALU.mult).then_inc(h_normed, 1)

                def take_logits(t):
                    dve.wait_ge(logits_done, t + 1)
                    if t == 0:
                        dve.wait_ge(const_in, 16 * len(consts))
                    own = v.tensor_tensor(logits[:, t, :], logit_bank[:, t % 2, 0:E], b_router[:], ALU.add)
                    own.then_inc(logits_read, 1)
                    dve.wait_ge(logits_read, t + 1)
                    link(v.max(out=top[:, t, :], in_=logits[:, t, :]))
                    link(v.max_index(out=top_i[:, t, :], in_max=top[:, t, :], in_values=logits[:, t, :]))

                dve.wait_ge(g_ffn_in, 16)
                v.memset(ones[:], 1.0)
                v.memset(before[:, 0, :], 0.0)
                for t in range(TILES + 1):
                    if t < TILES:
                        norm(t)
                    if t >= 1:
                        dve.wait_ge(xT_done, 2 * t)
                        if t >= 3:
                            dve.wait_ge(logits_done, t - 2)
                        v.tensor_copy(normT[:, (t - 1) % 2, 4:8, :].rearrange("p k q -> p (k q)"), xT_bank[:, 1, :])\
                            .then_inc(normT_hi, 1)
                    if t >= 2:
                        take_logits(t - 2)
                take_logits(TILES - 1)

                link(v.tensor_copy(top_f[:], top_i[:, :, 0:TOPK]))
                v.tensor_tensor(gates[:], top[:, :, 0:TOPK],
                                top[:, :, 0:1].to_broadcast([P, TILES, TOPK]), ALU.subtract).then_inc(gate_diff, 1)
                for k in range(TOPK):
                    last = v.tensor_tensor(chosen[:, k], repeat(expert_no[:], TILES), spread(top_f[:, :, k], E),
                                           ALU.is_equal)
                link(last)
                v.tensor_tensor(sel[:], chosen[:, 0], chosen[:, 1], ALU.add)
                link(v.tensor_tensor(picked[:, 0], chosen[:, 2], chosen[:, 3], ALU.add))
                link(v.tensor_tensor(sel[:], sel[:], picked[:, 0], ALU.add))
                for t in range(TILES):
                    last = v.tensor_tensor(before[:, t + 1, :], before[:, t, :], sel[:, t, :], ALU.add)
                    if t < TILES - 1:
                        link(last)
                last.then_inc(sel_ready, 1)
                dve.wait_ge(gate_exp, 1)
                link(v.tensor_reduce(gate_sum[:], gates[:], AX.X, ALU.add))
                link(v.reciprocal(gate_sum[:], gate_sum[:]))
                link(v.tensor_tensor(gates[:], gates[:], spread(gate_sum[:], TOPK), ALU.mult))

                dve.wait_ge(ranked, 1)
                link(v.tensor_scalar(blocks[:], count_bank[:, 0:E], 0.0, None, ALU.is_gt))
                for r in range(1, ROUNDS):
                    link(v.scalar_tensor_tensor(blocks[:], count_bank[:, 0:E], float(r * SLOTS), blocks[:],
                                                ALU.is_gt, ALU.add))
                link(v.tensor_tensor_scan(block_end[:], ones[:, 0:E], blocks[:], 0.0, ALU.mult, ALU.add))
                link(v.tensor_tensor(first_slot[:], block_end[:], blocks[:], ALU.subtract))
                link(v.tensor_scalar(first_slot[:], first_slot[:], float(SLOTS), float(SLOTS), ALU.mult, ALU.add))
                link(v.tensor_tensor(slot[:], rank_bank[:, 0:TILES * E].rearrange("p (t e) -> p t e", e=E),
                                     repeat(first_slot[:], TILES), ALU.add))
                for k in range(TOPK):
                    last = v.tensor_tensor(picked[:, k], chosen[:, k], slot[:], ALU.mult)
                link(last)
                for k in range(TOPK):
                    last = v.tensor_reduce(slot_f[:, k, :], picked[:, k], AX.X, ALU.add)
                link(last)
                v.tensor_copy(slot_i[:], slot_f[:]).then_inc(slots_ready, 1)
                link(v.tensor_tensor(past[:], repeat(block_end[:], BLOCKS + 1), spread(block_no[:], E), ALU.is_le))
                link(v.tensor_reduce(owner[:], past[:], AX.X, ALU.add))
                v.tensor_scalar(keep["owner_i"][:], owner[:], float(E - 1), None, ALU.min)
                link(v.tensor_tensor(end_slot[:], first_slot[:], count_bank[:, 0:E], ALU.add))
                link(v.tensor_tensor(past[:], repeat(expert_no[:], BLOCKS + 1), spread(owner[:], E), ALU.is_equal))
                link(v.tensor_tensor(past[:], past[:], repeat(end_slot[:], BLOCKS + 1), ALU.mult))
                link(v.tensor_reduce(filled[:], past[:], AX.X, ALU.add))
                link(v.scalar_tensor_tensor(filled[:], block_no[:], -float(SLOTS), filled[:], ALU.mult, ALU.add))
                link(v.tensor_scalar(filled[:], filled[:], -float(SLOTS), None, ALU.add))
                link(v.tensor_scalar(width_no[:], filled[:], float(WIDTHS[0]), None, ALU.is_gt))
                for width in WIDTHS[1:-1]:
                    link(v.scalar_tensor_tensor(width_no[:], filled[:], float(width), width_no[:],
                                                ALU.is_gt, ALU.add))
                link(v.tensor_scalar(owner[:], owner[:], float(E), float(len(WIDTHS)), ALU.is_ge, ALU.mult))
                v.tensor_tensor(keep["width_i"][:], width_no[:], owner[:], ALU.add)
                link(v.tensor_copy(keep["blocks_i"][:], block_end[:, E - 1:E]))

            @block.tensor
            def _(pe):
                for t in range(TILES + 1):
                    if t < TILES:
                        pe.wait_ge(h_normed, t + 1)
                        for b, freed in ((0, normT_lo), (1, normT_hi)):
                            if t >= 1:
                                pe.wait_ge(freed, t)
                            for k in range(4):
                                c = (4 * b + k) * P
                                last = nc.tensor.transpose(xT_bank[:, b, k * P:(k + 1) * P],
                                                           normed[:, t % 2, c:c + P], ident[:])
                            last.then_inc(xT_done, 1)
                    if t >= 1:
                        pe.wait_ge(normT_lo, t)
                        pe.wait_ge(normT_hi, t)
                        if t == 1:
                            pe.wait_ge(const_in, 16 * len(consts))
                        if t >= 3:
                            pe.wait_ge(logits_read, t - 2)
                        for k in range(DC):
                            last = nc.tensor.matmul(logit_bank[:, (t - 1) % 2, 0:E], normT[:, (t - 1) % 2, k, :],
                                                    w_router[:, k, :], start=(k == 0), stop=(k == DC - 1))
                        last.then_inc(logits_done, 1)
                pe.wait_ge(sel_ready, 1)
                nc.tensor.matmul(rank_bank[:, 0:TILES * E], tri[:], sel[:].rearrange("p t e -> p (t e)"),
                                 start=True, stop=False)
                nc.tensor.matmul(rank_bank[:, 0:TILES * E], ones[:], before[:, 0:TILES, :].rearrange("p t e -> p (t e)"),
                                 start=False, stop=True)
                nc.tensor.matmul(count_bank[:, 0:E], ones[:], before[:, TILES, :], start=True, stop=True)\
                    .then_inc(ranked, 1)


def experts(nc, io, keep):
    with ExitStack() as ctx:
        m = Mem(nc, ctx)
        HF = FF // 2
        w_gate = m.sb("w_gate_sb", [P, 2, DC, HF])
        w_up = m.sb("w_up_sb", [P, 2, DC, HF])
        w_down = m.sb("w_down_sb", [P, 2, FC, D // 2])
        bias_rows = m.sb("bias_rows", [3 * FC, P])
        bias_gu = m.sb("bias_gu", [P, 2 * FC])
        bias_next = m.sb("bias_next", [P, FC])
        bias_down = m.sb("bias_down", [P, FC])
        slot_rows = m.sb("slot_rows", [HALF, 2], U32)
        x_rows = m.sb("x_rows", [HALF, 2, D])
        xT = m.sb("xT", [P, DC, SLOTS])
        g_in = m.sb("g_in", [P, 2, SLOTS])
        u_in = m.sb("u_in", [P, 2, SLOTS])
        sig = m.sb("sig", [P, 2, SLOTS])
        g_sig = m.sb("g_sig", [P, 2, SLOTS])
        hidden = m.sb("hidden", [P, FC, SLOTS])
        yT = m.sb("yT", [P, DC, SLOTS])
        y_rows = m.sb("y_rows", [HALF, 2, D])
        spare = m.sb("spare", [P, 8])
        g_bank = m.ps("g_bank", [P, 2, 512])
        u_bank = m.ps("u_bank", [P, 2, 512])
        act_bank = m.ps("act_bank_e", [P, 512])
        dve_bank = m.ps("dve_bank_e", [P, 512])
        down_bank = m.ps("down_bank", [P, 2, 512])
        ident = keep["ident"]

        gate_in = [m.sem(f"gate_in{i}") for i in range(2)]
        up_in = [m.sem(f"up_in{i}") for i in range(2)]
        down_in = [m.sem(f"down_in{i}") for i in range(2)]
        bias_in = m.sem("bias_in")
        slots_in = m.sem("slots_in")
        slots_seen = m.sem("slots_seen")
        spare_set = m.sem("spare_set")
        x_in = m.sem("x_in_e")
        x_done = [m.sem(f"x_done{i}") for i in range(2)]
        x_out = [m.sem(f"x_out{i}") for i in range(2)]
        y_done = [m.sem(f"y_done{i}") for i in range(2)]
        y_out = [m.sem(f"y_out{i}") for i in range(2)]
        gu_done = m.sem("gu_done")
        gu_read = m.sem("gu_read")
        g_ready = m.sem("g_ready")
        sig_ready = m.sem("sig_ready")
        g_sig_ready = m.sem("g_sig_ready")
        hidden_ready = m.sem("hidden_ready")
        down_done = m.sem("down_done")
        down_read = m.sem("down_read")
        bias_set = m.sem("bias_set")
        y_stored = m.sem("y_stored")
        y_zero = m.sem("y_zero")

        with nc.Block() as block:

            @block.sync
            def _(sp):
                def expert_of(b):
                    return sp.value_load(keep["owner_i"][0:1, bass.ds(b, 1)], min_val=0, max_val=E - 1)

                def load_biases(e):
                    for i, name in enumerate(("b_gate", "b_up", "b_down")):
                        sp.dma_start(bias_rows[i * FC:(i + 1) * FC, :],
                                     io[name][bass.ds(e, 1), :].rearrange("one (f p) -> (one f) p", p=P))\
                            .then_inc(bias_in, 16)

                def load(e, b=None):
                    for half in range(2):
                        c = slice(half * HF, (half + 1) * HF)
                        if b is not None:
                            sp.wait_ge(gu_done, b * FC + 4 * (half + 1))
                        for w, name, arrived in ((w_gate, "w_gate", gate_in), (w_up, "w_up", up_in)):
                            sp.dma_start(w[:, half], io[name][bass.ds(e, 1), :, c]
                                         .rearrange("one (k p) n -> p (one k) n", p=P)).then_inc(arrived[half], 16)
                    for half in range(2):
                        c = slice(half * HF, (half + 1) * HF)
                        if b is not None:
                            sp.wait_ge(down_done, b * DC + 4 * (half + 1))
                        sp.dma_start(w_down[:, half], io["w_down"][bass.ds(e, 1), :, c]
                                     .rearrange("one (k p) n -> p (one k) n", p=P)).then_inc(down_in[half], 16)

                count = sp.value_load(keep["blocks_i"][0:1, 0:1], min_val=1, max_val=BLOCKS)
                first = expert_of(0)
                load_biases(first)
                load(first)
                with sp.Fori(0, BLOCKS // GROUP) as group:
                    with sp.If(group * GROUP < count):
                        with sp.Fori(0, GROUP) as turn:
                            b = sp.snap(group * GROUP + turn)
                            e = expert_of(b + 1)
                            with sp.If(b < count):
                                sp.wait_ge(x_done[1], b * 2 + 2)
                                load_biases(e)
                            with sp.If(b + 1 < count):
                                load(e, b)
                        sp.nop()

            @block.gpsimd
            def _(pool):
                def gather(b):
                    pool.dma_start(slot_rows[:], io["slot_token_u"][bass.ds(b * SLOTS + SLOTS, SLOTS), :]
                                   .rearrange("(p j) one -> p (j one)", p=HALF)).then_inc(slots_in, 16)
                    pool.wait_ge(slots_in, b * 16 + 16)
                    nc.gpsimd.tensor_tensor(spare[:, 4:5], spare[:, 3:4], spare[:, 3:4], ALU.add)\
                        .then_inc(slots_seen, 1)
                    for j in range(2):
                        pool.indirect_dma_start(
                            out=x_rows[:, j, :], out_offset=None, in_=io["rows"],
                            in_offset=bass.IndirectOffsetOnAxis(ap=slot_rows[:, j:j + 1], axis=0),
                            bounds_check=last_token, oob_is_err=False).then_inc(x_in, 16)

                count = pool.value_load(keep["blocks_i"][0:1, 0:1], min_val=1, max_val=BLOCKS)
                last_token = pool.to_reg(SEQ - 1)
                nc.gpsimd.memset(spare[:, 3:4], 0.0).then_inc(spare_set, 1)
                pool.wait_ge(spare_set, 1)
                def store(b):
                    for out in y_out:
                        pool.wait_ge(out, b * 2 + 2)
                    pool.dma_start(io["y"][bass.ds(b * SLOTS, SLOTS), :].rearrange("(p j) d -> p j d", p=HALF),
                                   y_rows[:]).then_inc(y_stored, 16)

                gather(0)
                with pool.Fori(0, BLOCKS // GROUP) as group:
                    with pool.If(group * GROUP < count):
                        with pool.Fori(0, GROUP) as turn:
                            b = pool.snap(group * GROUP + turn)
                            with pool.If(b < count):
                                pool.wait_ge(slots_seen, b + 1)
                                pool.wait_ge(x_done[1], b * 2 + 2)
                                gather(b + 1)
                                store(b)
                        pool.nop()
                store(count)
                pool.wait_ge(y_stored, count * 16 + 16)

            @block.scalar
            def _(act):
                count = act.value_load(keep["blocks_i"][0:1, 0:1], min_val=1, max_val=BLOCKS)

                def x_copies(b):
                    for i in range(2):
                        act.wait_ge(x_done[0], b * 2 + (i + 1))
                        nc.scalar.copy(xT[:, 4 * i:4 * i + 2, :].rearrange("p k q -> p (k q)"),
                                       g_bank[:, i, 0:2 * SLOTS]).then_inc(x_out[0], 1)

                nc.scalar.copy(spare[:, 1:2], ident[:, 0:1]).then_inc(down_read, 2)
                nc.scalar.copy(spare[:, 0:1], ident[:, 0:1]).then_inc(y_out[0], 1)
                x_copies(0)

                def y_copy(turn, half):
                    act.wait_ge(y_done[0], turn * 2 + (2 - half))
                    nc.scalar.copy(y_rows[:, 0, half * 512:(half + 1) * 512], act_bank[0:HALF, :])\
                        .then_inc(y_out[0], 1)

                with act.Fori(0, BLOCKS // GROUP) as group:
                    with act.If(group * GROUP < count):
                        with act.Fori(0, GROUP) as turn:
                            b = act.snap(group * GROUP + turn)
                            with act.If(b < count):
                                for f in range(FC):
                                    act.wait_ge(g_ready, b * FC + (f + 1))
                                    nc.scalar.activation(sig[:, f % 2, :], g_in[:, f % 2, :], ACT.Sigmoid, scale=ALPHA)\
                                        .then_inc(sig_ready, 1)
                                    if f == 1:
                                        y_copy(b, 1)
                                x_copies(b + 1)
                                act.wait_ge(bias_set, b + 1)
                                for c in range(DC):
                                    act.wait_ge(down_done, b * DC + (c + 1))
                                    nc.scalar.activation(yT[:, c, :], down_bank[:, c % 2, 0:SLOTS], ACT.Identity,
                                                         bias=bias_down[:, c:c + 1]).then_inc(down_read, 1)
                                    if c == 5:
                                        act.wait_ge(y_stored, b * 16 + 16)
                                        y_copy(b, 0)
                        act.nop()
                y_copy(count, 1)

            @block.vector
            def _(dve):
                v = nc.vector
                count = dve.value_load(keep["blocks_i"][0:1, 0:1], min_val=1, max_val=BLOCKS)

                def x_copies(b):
                    for i in range(2):
                        dve.wait_ge(x_done[1], b * 2 + (i + 1))
                        if i == 0:
                            at = 2 * SLOTS
                            v.tensor_copy(bias_gu[:, 0:FC], u_bank[:, i, at:at + FC])
                            v.tensor_scalar(bias_gu[:, FC:2 * FC], u_bank[:, i, at + FC:at + 2 * FC], 1.0, None, ALU.add)
                            v.tensor_copy(bias_next[:], u_bank[:, i, at + 2 * FC:at + 3 * FC])
                        v.tensor_copy(xT[:, 4 * i + 2:4 * i + 4, :].rearrange("p k q -> p (k q)"),
                                      u_bank[:, i, 0:2 * SLOTS]).then_inc(x_out[1], 1)

                v.memset(spare[:, 2:3], 0.0).then_inc(gu_read, 2)
                v.memset(spare[:, 5:6], 0.0).then_inc(y_out[1], 1)
                v.memset(y_rows[:], 0.0)
                v.memset(yT[:], 0.0).then_inc(y_zero, 1)
                x_copies(0)

                def y_copy(turn, half):
                    dve.wait_ge(y_done[1], turn * 2 + (2 - half))
                    v.tensor_copy(y_rows[:, 1, half * 512:(half + 1) * 512], dve_bank[0:HALF, :])\
                        .then_inc(y_out[1], 1)

                with dve.Fori(0, BLOCKS // GROUP) as group:
                    with dve.If(group * GROUP < count):
                        with dve.Fori(0, GROUP) as turn:
                            b = dve.snap(group * GROUP + turn)
                            with dve.If(b < count):
                                dve.wait_ge(x_out[1], b * 2 + 2)
                                dve.wait_ge(down_read, b * DC + 2)
                                v.tensor_copy(bias_down[:], bias_next[:]).then_inc(bias_set, 1)
                                for f in range(FC + 1):
                                    if f < FC:
                                        dve.wait_ge(gu_done, b * FC + (f + 1))
                                        if f >= 2:
                                            dve.wait_ge(hidden_ready, b * FC + (f - 1))
                                        v.tensor_scalar(g_in[:, f % 2, :], g_bank[:, f % 2, 0:SLOTS], bias_gu[:, f:f + 1],
                                                        LIMIT, ALU.add, ALU.min).then_inc(g_ready, 1)
                                        v.tensor_scalar(u_in[:, f % 2, :], u_bank[:, f % 2, 0:SLOTS],
                                                        bias_gu[:, FC + f:FC + f + 1], 1.0 + LIMIT, ALU.add, ALU.min)\
                                            .then_inc(gu_read, 1)
                                    if f >= 1:
                                        s = f - 1
                                        dve.wait_ge(sig_ready, b * FC + f)
                                        v.tensor_tensor(g_sig[:, s % 2, :], g_in[:, s % 2, :], sig[:, s % 2, :], ALU.mult)\
                                            .then_inc(g_sig_ready, 1)
                                        dve.wait_ge(g_sig_ready, b * FC + f)
                                        v.scalar_tensor_tensor(hidden[:, s, :], u_in[:, s % 2, :], 1.0 - LIMIT, g_sig[:, s % 2, :],
                                                               ALU.max, ALU.mult).then_inc(hidden_ready, 1)
                                    if f == 2:
                                        y_copy(b, 1)
                                x_copies(b + 1)
                                dve.wait_ge(y_stored, b * 16 + 16)
                                y_copy(b, 0)
                        dve.nop()
                y_copy(count, 1)

            @block.tensor
            def _(pe):
                def transpose_x(b, last_b):
                    pe.wait_ge(x_in, b * 32 + 32)
                    pe.wait_ge(bias_in, b * 48 + 48)
                    for x in range(4):
                        i, reader = divmod(x, 2)
                        bank = (g_bank, u_bank)[reader]
                        if reader == 0 and last_b is not None:
                            pe.wait_ge(gu_read, last_b * FC + (FC + 1 + i))
                        for c in range(2):
                            for j in range(2):
                                at, k = (2 * c + j) * HALF, 2 * x + c
                                last = nc.tensor.transpose(bank[:, i, at:at + HALF], x_rows[:, j, k * P:(k + 1) * P],
                                                           ident[0:HALF, 0:HALF])
                        if x == 1:
                            at = 2 * SLOTS
                            last = nc.tensor.transpose(bank[:, i, at:at + 3 * FC], bias_rows[:],
                                                       ident[0:3 * FC, 0:3 * FC])
                        last.then_inc(x_done[reader], 1)

                def transpose_y(turn, half):
                    banks = (act_bank, dve_bank)
                    read = turn * DC + (1 if half else 5)
                    pe.wait_ge(down_read, read)
                    for j in range(2):
                        pe.wait_ge(y_out[j], turn * 2 + (2 - half))
                    for k in range(4):
                        if k == 3:
                            pe.wait_ge(down_read, read + 1)
                        for j, bank in enumerate(banks):
                            last = nc.tensor.transpose(bank[0:HALF, k * P:(k + 1) * P],
                                                       yT[:, 4 * half + k, j * HALF:(j + 1) * HALF], ident[:])
                            if k == 3:
                                last.then_inc(y_done[j], 1)

                def products(b, width):
                    n = width // 2

                    def taken(ap):
                        return ap.rearrange("p (j s) -> p j s", j=2)[:, :, 0:n]

                    for out in x_out:
                        pe.wait_ge(out, b * 2 + 2)
                    for f in range(FC):
                        half, c = divmod(f, FC // 2)
                        if c == 0:
                            pe.wait_ge(gate_in[half], b * 16 + 16)
                            pe.wait_ge(up_in[half], b * 16 + 16)
                        pe.wait_ge(gu_read, b * FC + (f + 1))
                        for w, bank in ((w_gate, g_bank), (w_up, u_bank)):
                            for k in range(DC):
                                last = nc.tensor.matmul(taken(bank[:, f % 2, 0:SLOTS]),
                                                        w[:, half, k, c * P:(c + 1) * P], taken(xT[:, k, :]),
                                                        start=(k == 0), stop=(k == DC - 1))
                        last.then_inc(gu_done, 1)
                        if f == 0:
                            transpose_y(b, 1)
                            pe.load(next_no, keep["width_i"][0:1, bass.ds(b + 1, 1)])
                    transpose_x(b + 1, b)
                    pe.wait_ge(hidden_ready, b * FC + (FC - 1))
                    for c in range(DC):
                        half, c4 = divmod(c, DC // 2)
                        if c4 == 0:
                            pe.wait_ge(down_in[half], b * 16 + 16)
                        pe.wait_ge(down_read, b * DC + (c + 1))
                        for k in range(FC):
                            if c == 0 and k == FC - 1:
                                pe.wait_ge(hidden_ready, b * FC + FC)
                            last = nc.tensor.matmul(taken(down_bank[:, c % 2, 0:SLOTS]),
                                                    w_down[:, half, k, c4 * P:(c4 + 1) * P], taken(hidden[:, k, :]),
                                                    start=(k == 0), stop=(k == FC - 1))
                        last.then_inc(down_done, 1)
                        if c == 4:
                            transpose_y(b, 0)

                for bank in (g_bank, u_bank, down_bank):
                    for i in range(2):
                        nc.tensor.matmul(bank[:, i, WIDTHS[0] // 2:SLOTS], ident[:], ident[:, 0:SLOTS - WIDTHS[0] // 2],
                                         start=True, stop=True)
                def choose(b, width_no, lo, hi):
                    if hi - lo == 1:
                        products(b, WIDTHS[lo])
                        return
                    mid = (lo + hi) // 2
                    with pe.If_lt(width_no, mid):
                        choose(b, width_no, lo, mid)
                    with pe.Else():
                        choose(b, width_no, mid, hi)
                    pe.nop()

                transpose_x(0, None)
                pe.wait_ge(y_zero, 1)
                count = pe.value_load(keep["blocks_i"][0:1, 0:1], min_val=1, max_val=BLOCKS)
                this_no, next_no = pe.alloc_register("this_no"), pe.alloc_register("next_no")
                pe.load(next_no, keep["width_i"][0:1, 0:1])
                with pe.Fori(0, BLOCKS // GROUP) as group:
                    with pe.If(group * GROUP < count):
                        with pe.Fori(0, GROUP) as turn:
                            b = pe.snap(group * GROUP + turn)
                            with pe.If(b < count):
                                pe.reg_mov(this_no, next_no)
                                choose(b, this_no, 0, len(WIDTHS))
                        pe.nop()
                transpose_y(count, 1)

def combine(nc, io, keep):
    with ExitStack() as ctx:
        m = Mem(nc, ctx)
        picked = m.sb("picked_c", [P, TILES, TOPK, D])
        acc = keep["h"]
        rows_in = [m.sem(f"rows_in{t}") for t in range(TILES)]
        added = m.sem("added")
        summed = m.sem("summed")
        out_stored = m.sem("out_stored")

        with nc.Block() as block:

            @block.sync
            def _(sp):
                for t in range(TILES):
                    sp.wait_ge(summed, t + 1)
                    sp.dma_start(io["out"][0, t * P:(t + 1) * P, :], acc[:, t, :]).then_inc(out_stored, 16)
                sp.wait_ge(out_stored, 16 * TILES)

            @block.gpsimd
            def _(pool):
                for t in range(TILES):
                    for k in range(TOPK):
                        pool.indirect_dma_start(
                            out=picked[:, t, k, :], out_offset=None, in_=io["y"],
                            in_offset=bass.IndirectOffsetOnAxis(ap=keep["slot_i"][:, k, t:t + 1], axis=0),
                            bounds_check=(BLOCKS + 1) * SLOTS - 1, oob_is_err=False).then_inc(rows_in[t], 16)

            @block.vector
            def _(dve):
                for t in range(TILES):
                    dve.wait_ge(rows_in[t], 16 * TOPK)
                    for k in range(TOPK):
                        if k:
                            dve.wait_ge(added, (TOPK - 1) * t + k)
                        nc.vector.scalar_tensor_tensor(acc[:, t, :], picked[:, t, k, :],
                                                       keep["gates"][:, t, k:k + 1], acc[:, t, :],
                                                       ALU.mult, ALU.add).then_inc(added if k < TOPK - 1 else summed, 1)


def program(nc, io):
    with ExitStack() as ctx:
        m = Mem(nc, ctx)
        keep = {
            "ident": m.sb("ident_sb", [P, P]),
            "eps": m.sb("eps", [P, 1]),
            "act_own": m.sem("act_own_r"),
        }
        with nc.Block() as block:

            @block.vector
            def _(dve):
                nc.vector.memset(keep["eps"][:], EPS)

        with ExitStack() as attention:
            m = Mem(nc, attention)
            keep["swa_qT"] = m.sb("swa_qT", [P, PAIRS, SEQ])
            keep["swa_kT"] = m.sb("swa_kT", [P, KEYS])
            keep["swa_v"] = m.sb("swa_v", [P, MT + 1, SWA_KV * HD])
            keep["mla_qT"] = m.sb("mla_qT", [QK, MLA_HEADS, SEQ])
            keep["mla_kT"] = m.sb("mla_kT", [QK, MLA_HEADS, KEYS])
            keep["mla_v"] = m.sb("mla_v", [P, MT + 1, MLA_HEADS, VD])
            project(nc, io, keep)
            attend(nc, io, keep)
        m = Mem(nc, ctx)
        keep["h"] = m.sb("h_sb", [P, TILES, D])
        keep["gates"] = m.sb("gates", [P, TILES, TOPK])
        keep["slot_i"] = m.sb("slot_i", [P, TOPK, TILES], U32)
        keep["owner_i"] = m.sb("owner_i", [P, BLOCKS + 1], I32)
        keep["width_i"] = m.sb("width_i", [P, BLOCKS + 1], I32)
        keep["blocks_i"] = m.sb("blocks_i", [P, 1], I32)
        route(nc, io, keep)
        experts(nc, io, keep)
        combine(nc, io, keep)


def constants():
    import numpy as np

    f = np.float32
    row, col = np.arange(P)[:, None], np.arange(P)[None, :]
    pos = np.zeros((P, MT + 1), f)
    for t in range(TILES):
        pos[:, t] = META + t * P + np.arange(P)
    pos[:META, MT] = np.arange(META)
    half = ROPE // 2
    inv = (1.0 / (f(10000.0) ** (np.arange(half, dtype=f) / f(half)))).astype(f)
    angle = (pos[:, :, None] * inv).astype(f)
    cos, sin = np.cos(angle).astype(f), np.sin(angle).astype(f)
    band = np.empty((P, SWA_HEADS, BAND), f)
    for h in range(SWA_HEADS):
        slope = f(2.0 ** (-8.0 * (h + 1) / SWA_HEADS))
        for c0, shift in ((0, -P), (P + META, 0), (2 * P + META, P)):
            dist = np.abs(row - (col + shift))
            band[:, h, c0:c0 + P] = np.where(dist <= P, -slope * dist.astype(f), f(-1e30))
        band[:, h, P:P + META] = 0.0
    inv_n = np.array([1 / HD] * 10 + [1 / Q_LORA, 1 / KV_LORA], f)
    return {
        "ident": np.eye(P, dtype=f),
        "tri": (row < col).astype(f),
        "cos2": np.concatenate([cos, cos], 2),
        "sin2": np.concatenate([-sin, sin], 2),
        "band_bias": band,
        "inv_n": np.tile(inv_n, (P, 1)),
        "expert_no": np.tile(np.arange(E, dtype=f), (P, 1)),
        "block_no": np.tile(np.arange(BLOCKS + 1, dtype=f), (P, 1)),
        "token_no": (np.arange(TILES)[None, :] * P + np.arange(P)[:, None]).astype(np.int32),
    }


def kernel(**inputs):
    import numpy as np
    import concourse.bacc as bacc
    from concourse.bass_utils import run_bass_kernel_spmd

    nc = bacc.Bacc("TRN2", target_bir_lowering=False, num_devices=1)
    arrays, io = {}, {}
    for name, a in {**inputs, **constants()}.items():
        a = np.ascontiguousarray(a)
        if name in ("w_gate", "w_up", "w_down", "b_gate", "b_up", "b_down"):
            a = a[0]
        arrays["in_" + name] = a
        io[name] = nc.dram_tensor("in_" + name, a.shape, mybir.dt.from_np(a.dtype), kind="ExternalInput").ap()
    io["out"] = nc.dram_tensor("out_y", (1, SEQ, D), F32, kind="ExternalOutput").ap()
    io["h"] = nc.dram_tensor("residual", (SEQ, D), F32).ap()
    io["rows"] = nc.dram_tensor("ffn_rows", (SEQ, D), F32).ap()
    io["y"] = nc.dram_tensor("expert_rows", ((BLOCKS + 1) * SLOTS, D), F32).ap()
    table = nc.dram_tensor("slot_token", ((BLOCKS + 2) * SLOTS, 1), I32).ap()
    io["slot_token"], io["slot_token_u"] = table, table.bitcast(U32)
    program(nc, io)
    result = run_bass_kernel_spmd(nc, [arrays], core_ids=[0])
    return result.results[0]["out_y"]
```
